# Optimizing a Trainium2 kernel written in Bass

```python
import math
import jax, jax.numpy as jnp
from jax import lax
import numpy as np

D_MODEL = 1024
BATCH = 1
SEQ = 256
DEPTH = 1

CHUNK = 64
Q_BLOCK = 128
POOL_WINDOWS = (2, 4, 8, 16)
N_POOL_GROUPS = len(POOL_WINDOWS)
POOL_WIDTH = D_MODEL // 2
POOL_GROUP = POOL_WIDTH // N_POOL_GROUPS
N_HEADS = 4
HEAD_DIM = D_MODEL // 16
V_HEAD_DIM = 2 * HEAD_DIM
QK_WIDTH = N_HEADS * 2 * HEAD_DIM
ATTN_WIDTH = N_HEADS * V_HEAD_DIM
ROT_DIM = HEAD_DIM // 4
ROPE_THETA = 500000.0
N_BRANCHES = 2
IN_WIDTH = POOL_WIDTH + 2 * QK_WIDTH + ATTN_WIDTH + N_BRANCHES * D_MODEL
N_EXPERTS = 32
TOP_K = 4
D_EXPERT = D_MODEL
SWIGLU_LIMIT = 7.0
SWIGLU_ALPHA = 1.702
NORM_EPS = 1e-6

kernel_name = "hybrid_pool_diffattn_moe_block"

def rmsnorm(x, g, eps=NORM_EPS):
    xf = x.astype(jnp.float32)
    y = xf * lax.rsqrt(jnp.mean(xf * xf, axis=-1, keepdims=True) + eps)
    return (y * g.astype(jnp.float32)).astype(x.dtype)

def rotary_tables(seq):
    inv_freq = ROPE_THETA ** (-jnp.arange(0, ROT_DIM, 2, dtype=jnp.float32) / ROT_DIM)
    ang = jnp.arange(seq, dtype=jnp.float32)[:, None] * inv_freq[None, :]
    return jnp.cos(ang), jnp.sin(ang)

def apply_partial_rotary(t, cos, sin):
    half = ROT_DIM // 2
    c = cos[None, :, None, None, :].astype(t.dtype)
    s = sin[None, :, None, None, :].astype(t.dtype)
    t1 = t[..., :half]
    t2 = t[..., half:ROT_DIM]
    return jnp.concatenate([t1 * c - t2 * s, t2 * c + t1 * s, t[..., ROT_DIM:]], axis=-1)

def multiscale_pool(u, w_grp, scale):
    b, s, _ = u.shape
    uf = u.astype(jnp.float32)
    count = jnp.arange(1, s + 1, dtype=jnp.float32)[None, :, None]
    outs = []
    for gi, w in enumerate(POOL_WINDOWS):
        ug = uf[..., gi * POOL_GROUP:(gi + 1) * POOL_GROUP]
        c = jnp.cumsum(ug, axis=1)
        c_lag = jnp.pad(c, ((0, 0), (w, 0), (0, 0)))[:, :s]
        mean = (c - c_lag) / jnp.minimum(count, float(w))
        outs.append(mean - ug)
    p = jnp.stack(outs, axis=2).astype(u.dtype)
    y = jnp.einsum('bsgc,gcd->bsgd', p, w_grp).reshape(b, s, POOL_WIDTH)
    return y * scale

def diff_attention(q, k, v, lam):
    s = q.shape[1]
    sm_scale = HEAD_DIM ** -0.5
    chunk_id = jnp.arange(s) // CHUNK
    outs = []
    for i in range(s // Q_BLOCK):
        lo, hi = i * Q_BLOCK, (i + 1) * Q_BLOCK
        qb = q[:, lo:hi]
        kb = k[:, :hi]
        vb = v[:, :hi]
        sc = jnp.einsum('bqhmd,bkhmd->bhmqk', qb, kb).astype(jnp.float32) * sm_scale
        mask = chunk_id[lo:hi, None] >= chunk_id[None, :hi]
        sc = jnp.where(mask[None, None, None], sc, -jnp.inf)
        p = jax.nn.softmax(sc, axis=-1)
        a = p[:, :, 0] - lam * p[:, :, 1]
        outs.append(jnp.einsum('bhqk,bkhd->bqhd', a.astype(v.dtype), vb))
    return jnp.concatenate(outs, axis=1)

def moe_ffn(h, router_w, router_b, w_gate, b_gate, w_up, b_up, w_down, b_down):
    b, s, d = h.shape
    t = h.reshape(-1, d)
    logits = (t @ router_w + router_b).astype(jnp.float32)
    top_v, top_i = lax.top_k(logits, TOP_K)
    top_p = jax.nn.softmax(top_v, axis=-1)
    comb = jnp.sum(jax.nn.one_hot(top_i, N_EXPERTS, dtype=jnp.float32) * top_p[..., None], axis=1)
    comb = comb.astype(h.dtype)
    out = jnp.zeros_like(t)
    for e in range(N_EXPERTS):
        g = jnp.minimum(t @ w_gate[e] + b_gate[e], SWIGLU_LIMIT)
        u = jnp.clip(t @ w_up[e] + b_up[e], -SWIGLU_LIMIT, SWIGLU_LIMIT)
        act = (u + 1.0) * (g * jax.nn.sigmoid(SWIGLU_ALPHA * g))
        out = out + comb[:, e:e + 1] * (act @ w_down[e] + b_down[e])
    return out.reshape(b, s, d)

def setup_inputs(seed: int = 0) -> dict:
    key = jax.random.key(seed)
    ks = jax.random.split(key, 26)
    f32 = jnp.float32
    nrm = lambda k, shape, sc: jax.random.normal(k, shape, f32) * sc
    L, D, E, F = DEPTH, D_MODEL, N_EXPERTS, D_EXPERT
    return {
        "x": nrm(ks[0], (BATCH, SEQ, D), 1.0),
        "mix_norm_g": 1.0 + nrm(ks[1], (L, D), 0.05),
        "w_in": nrm(ks[2], (L, D, IN_WIDTH), D ** -0.5),
        "b_branch_gate": nrm(ks[3], (L, N_BRANCHES * D), 0.02),
        "pool_w": nrm(ks[4], (L, N_POOL_GROUPS, POOL_GROUP, POOL_GROUP), POOL_GROUP ** -0.5),
        "pool_scale": 1.0 + nrm(ks[5], (L, POOL_WIDTH), 0.1),
        "pool_up": nrm(ks[6], (L, POOL_WIDTH, D), POOL_WIDTH ** -0.5),
        "q_norm_g": 1.0 + nrm(ks[7], (L, HEAD_DIM), 0.05),
        "k_norm_g": 1.0 + nrm(ks[8], (L, HEAD_DIM), 0.05),
        "lambda_q1": nrm(ks[9], (L, HEAD_DIM), 0.1),
        "lambda_k1": nrm(ks[10], (L, HEAD_DIM), 0.1),
        "lambda_q2": nrm(ks[11], (L, HEAD_DIM), 0.1),
        "lambda_k2": nrm(ks[12], (L, HEAD_DIM), 0.1),
        "subln_g": 1.0 + nrm(ks[13], (L, V_HEAD_DIM), 0.05),
        "attn_up": nrm(ks[14], (L, ATTN_WIDTH, D), ATTN_WIDTH ** -0.5),
        "w_out": nrm(ks[15], (L, D, D), D ** -0.5),
        "ffn_norm_g": 1.0 + nrm(ks[16], (L, D), 0.05),
        "router_w": nrm(ks[17], (L, D, E), D ** -0.5),
        "router_b": nrm(ks[18], (L, E), 0.01),
        "exp_w_gate": nrm(ks[19], (L, E, D, F), D ** -0.5),
        "exp_b_gate": nrm(ks[20], (L, E, F), 0.02),
        "exp_w_up": nrm(ks[21], (L, E, D, F), D ** -0.5),
        "exp_b_up": nrm(ks[22], (L, E, F), 0.02),
        "exp_w_down": nrm(ks[23], (L, E, F, D), F ** -0.5),
        "exp_b_down": nrm(ks[24], (L, E, D), 0.02),
    }

def reference(x, mix_norm_g, w_in, b_branch_gate, pool_w, pool_scale, pool_up, q_norm_g, k_norm_g,
              lambda_q1, lambda_k1, lambda_q2, lambda_k2, subln_g, attn_up, w_out, ffn_norm_g,
              router_w, router_b, exp_w_gate, exp_b_gate, exp_w_up, exp_b_up, exp_w_down, exp_b_down):
    b, s, d = x.shape
    cos, sin = rotary_tables(s)
    o_q = POOL_WIDTH
    o_k = o_q + QK_WIDTH
    o_v = o_k + QK_WIDTH
    o_g = o_v + ATTN_WIDTH
    for l in range(DEPTH):
        h = rmsnorm(x, mix_norm_g[l])
        proj = h @ w_in[l]
        u_pool = proj[..., :o_q]
        q = proj[..., o_q:o_k].reshape(b, s, N_HEADS, 2, HEAD_DIM)
        k = proj[..., o_k:o_v].reshape(b, s, N_HEADS, 2, HEAD_DIM)
        v = proj[..., o_v:o_g].reshape(b, s, N_HEADS, V_HEAD_DIM)
        gates = jax.nn.sigmoid(proj[..., o_g:] + b_branch_gate[l])
        g_pool, g_attn = gates[..., :d], gates[..., d:]

        y_pool = multiscale_pool(u_pool, pool_w[l], pool_scale[l]) @ pool_up[l]

        q = apply_partial_rotary(rmsnorm(q, q_norm_g[l]), cos, sin)
        k = apply_partial_rotary(rmsnorm(k, k_norm_g[l]), cos, sin)
        lam_init = 0.8 - 0.6 * math.exp(-0.3 * l)
        lam = (jnp.exp(jnp.sum(lambda_q1[l].astype(jnp.float32) * lambda_k1[l].astype(jnp.float32)))
               - jnp.exp(jnp.sum(lambda_q2[l].astype(jnp.float32) * lambda_k2[l].astype(jnp.float32)))
               + lam_init)
        o = diff_attention(q, k, v, lam)
        o = rmsnorm(o, subln_g[l]) * (1.0 - lam_init)
        y_attn = o.reshape(b, s, ATTN_WIDTH) @ attn_up[l]

        merged = g_pool * y_pool + g_attn * y_attn
        x = x + merged @ w_out[l]

        h2 = rmsnorm(x, ffn_norm_g[l])
        x = x + moe_ffn(h2, router_w[l], router_b[l], exp_w_gate[l], exp_b_gate[l],
                        exp_w_up[l], exp_b_up[l], exp_w_down[l], exp_b_down[l])
    return x


_drawn_inputs = setup_inputs


def setup_inputs(seed=0):
    import zlib

    import numpy as np

    out = dict(_drawn_inputs(seed))
    spreads = {}
    factors = {'b_branch_gate': 3.16,
     'lambda_k1': 5.419,
     'exp_b_gate': 7.054,
     'exp_b_up': 8.0,
     'exp_b_down': 6.691}
    for name, (base, spread) in spreads.items():
        noise = np.random.default_rng([zlib.crc32(name.encode()), seed]).standard_normal(out[name].shape)
        drawn = base * np.exp(spread * noise) if base else spread * noise
        out[name] = __import__('jax').numpy.asarray(drawn.astype(out[name].dtype))
    for name, factor in factors.items():
        out[name] = (out[name] * factor).astype(out[name].dtype)
    return out
```

```python
from contextlib import ExitStack

import numpy as np

import concourse.bass as bass
from concourse import mybir

ALU = mybir.AluOpType
ACT = mybir.ActivationFunctionType
AX = mybir.AxisListType
F32 = mybir.dt.float32
I32 = mybir.dt.int32
U32 = mybir.dt.uint32

P = 128
D = 1024
S = 256
NT = S // P
NC = D // P
HEADS, HD, VD = 4, 64, 128
QK = HEADS * 2 * HD
POOLW = 512
NG = 4
PAD = 16
CHUNK = 64
ROT = HD // 4
E = 32
TOPK = 4
F = 1024
EPS = 1e-6
LIMIT, ALPHA = 7.0, 1.702
LAM_INIT = 0.8 - 0.6
MASKED = -1e30

HALF = 512
SLOTS = 8
PIECE = NC * HALF
BLOCK = 64
ROUNDS = S // BLOCK
UNROLL = 4
STEPS = E // UNROLL
PIECES_PER_EXPERT = 6

C_IDENT, C_TRI, C_ONES, C_IOTA, C_INV, C_COS, C_SIN, C_MASKQ, C_MASKK = 0, 128, 256, 384, 448, 512, 528, 544, 672
C_WIDTH = 736
R_MIXG, R_BGATE, R_PSCALE, R_SUBLN, R_FFNG, R_ROWS = 0, 8, 24, 28, 29, 37


def shape_constants():
    c = np.zeros((P, C_WIDTH), np.float32)
    c[:, C_IDENT:C_IDENT + P] = np.eye(P)
    c[:, C_TRI:C_TRI + P] = np.triu(np.ones((P, P)))
    c[:, C_ONES:C_ONES + P] = 1.0
    c[:, C_IOTA:C_IOTA + BLOCK] = np.arange(BLOCK)
    for g in range(NG):
        c[:, C_INV + 16 * g:C_INV + 16 * (g + 1)] = 1.0 / np.minimum(np.arange(1, 17), 2 << g)
    inv = (np.float32(500000.0) ** (-np.arange(0, ROT, 2, dtype=np.float32) / np.float32(ROT))).astype(np.float32)
    ang = np.arange(S, dtype=np.float32)[:, None] * inv[None, :]
    for t in range(NT):
        c[:, C_COS + 8 * t:C_COS + 8 * t + 8] = np.cos(ang[P * t:P * (t + 1)])
        c[:, C_SIN + 8 * t:C_SIN + 8 * t + 8] = np.sin(ang[P * t:P * (t + 1)])
    c[0, C_MASKQ:C_MASKQ + CHUNK] = 1.0
    c[0, C_MASKK:C_MASKK + CHUNK] = MASKED
    return c


def build(nc, A, consts, out):
    with ExitStack() as ctx:
        def sb(name, shape, dt=F32):
            return ctx.enter_context(nc.sbuf_tensor(name, shape, dt))

        def sem(name):
            return ctx.enter_context(nc.semaphore(name))

        ps = ctx.enter_context(nc.psum_tensor("ps", [P, 8, HALF], F32))

        ring = sb("ring", [P, SLOTS, PIECE])
        xt = sb("xt", [P, NT, D])
        qk_tok = xt[:].rearrange("p t (w c) -> p w t c", w=2)
        con = sb("con", [P, C_WIDTH])
        cols = sb("cols", [P, R_ROWS])
        small = sb("small", [P, 256])
        arena = sb("arena", [P, 16400])
        ident = con[:, C_IDENT:C_IDENT + P]
        tri = con[:, C_TRI:C_TRI + P]
        ones = con[:, C_ONES:C_ONES + P]
        iota = con[:, C_IOTA:C_IOTA + BLOCK]

        taken = [0]

        def part(n):
            at = taken[0]
            taken[0] += n
            assert taken[0] <= 16400, taken[0]
            return arena[:, at:at + n]

        hT = part(NC * S).rearrange("p (c s) -> p c s", c=NC)
        qT = part(HEADS * S).rearrange("p (h s) -> p h s", h=HEADS)
        kT = part(HEADS * S).rearrange("p (h s) -> p h s", h=HEADS)
        gate = part(2 * NC * S).rearrange("p (c s) -> p c s", c=2 * NC)
        vtok = part(NT * 512).rearrange("p (t c) -> p t c", t=NT)
        uT = part(NG * (S + PAD)).rearrange("p (g s) -> p g s", g=NG)
        pT = part(NG * S).rearrange("p (g s) -> p g s", g=NG)
        sums = part(2 * (S + PAD)).rearrange("p (b s) -> p b s", b=2)
        prob = part(2 * 2 * S).rearrange("p (b m s) -> p b m s", b=2, m=2)
        diff = part(2 * S).rearrange("p (b s) -> p b s", b=2)
        diffT = part(2 * S).rearrange("p (b s) -> p b s", b=2)
        otok_flat = part(NT * 512)
        otok = otok_flat.rearrange("p (t c) -> p t c", t=NT)
        oT = qT
        yT = uT[:, :, PAD:]
        prow = otok_flat[:, 0:P]
        lamv = otok_flat[:, P:P + 4 * HD].rearrange("p (i d) -> p i d", i=4)
        squares = prob.rearrange("p b m s -> p b (m s)")
        junk = gate[:, NC:, :].rearrange("p (t c) s -> p t (c s)", t=NT)
        first_end = taken[0]
        gq = part(HD)
        gk = part(HD)
        poolw = part(NG * P).rearrange("p (g d) -> p g d", g=NG)
        rw = part(NC * E).rearrange("p (c e) -> p c e", c=NC)
        rb = part(E)
        h2 = hT.rearrange("p c s -> p (c s)").rearrange("p (t d) -> p t d", t=NT)
        taken[0] = NC * S
        h2T = part(NC * S).rearrange("p (c s) -> p c s", c=NC)
        h_in = part(2 * NC * BLOCK).rearrange("p (b c h s) -> p b c h s", b=2, c=4, h=2)
        h_got = part(HALF)
        g1 = part(HALF)
        sig = part(HALF)
        gs = part(HALF)
        u1 = part(HALF)
        act_out = part(HALF)
        actT = part(NC * BLOCK).rearrange("p (c h s) -> p c h s", c=4, h=2)
        y_e = part(HALF)
        pickT = part(S)
        pick = part(2 * NT * BLOCK).rearrange("p (b t s) -> p b t s", b=2, t=NT)
        pickw = part(2 * NT * 2 * BLOCK).rearrange("p (b t h s) -> p b t h s", b=2, t=NT, h=2)
        this_e = part(2 * 2 * BLOCK).rearrange("p (b k s) -> p b k s", b=2, k=2)
        bias_rows = part(D)
        rank_tab = part(NT * (ROUNDS + 1) * E).rearrange("p (t n) -> p t n", t=NT)
        comb_tab = part(NT * (ROUNDS + 1) * E).rearrange("p (t n) -> p t n", t=NT)
        combT = part(S)
        eq4 = part(TOPK * E).rearrange("p (k e) -> p k e", k=TOPK)
        eq4w = part(TOPK * E).rearrange("p (k e) -> p k e", k=TOPK)
        logit = part(NT * E).rearrange("p (t e) -> p t e", t=NT)
        chosen = part(NT * E).rearrange("p (t e) -> p t e", t=NT)
        combf = part(NT * E).rearrange("p (t e) -> p t e", t=NT)
        ranks = part(NT * E).rearrange("p (t e) -> p t e", t=NT)
        bdown = part(D)[0:E, :]
        assert taken[0] <= first_end, (taken[0], first_end)
        top = sb("top", [P, NT, 8])
        topi = sb("topi", [P, NT, 8], U32)
        topf = sb("topf", [P, NT, 8])
        topw = sb("topw", [P, NT, TOPK])
        junk_o = sb("junk_o", [P, VD])
        rounds_i = sb("rounds_i", [1, 1], I32)

        ss = small[:, 0:2]
        rstd = small[:, 2:4]
        qss = small[:, 8:40].rearrange("p (i g) -> p i g", i=4)
        qrs = small[:, 40:72].rearrange("p (i g) -> p i g", i=4)
        lam2 = small[:, 136:138]
        neglam = small[:, 138:139]
        mx = small[:, 140:144].rearrange("p (b m) -> p b m", b=2)
        den = small[:, 144:148].rearrange("p (b m) -> p b m", b=2)
        oss = small[:, 152:160]
        ors = small[:, 160:168]
        ngate = small[:, 168:184]
        subln8 = small[:, 184:185]
        nmax = small[:, 186:188]
        psum4 = small[:, 188:190]
        cnt = small[0:1, 192:193]
        cnt2 = small[0:1, 194:196]
        ropeb = sb("ropeb", [P, 8, 16])

        params = ([(gq, A["q_norm_g"][0:1, :].broadcast_to([P, A["q_norm_g"].shape[1]])), (gk, A["k_norm_g"][0:1, :].broadcast_to([P, A["k_norm_g"].shape[1]]))]
                  + [(lamv[:, i, :], A[n][0:1, :].broadcast_to([P, HD]))
                     for i, n in enumerate(("lambda_q1", "lambda_q2", "lambda_k1", "lambda_k2"))]
                  + [(poolw, A["pool_w"][0].rearrange("g c d -> c g d")),
                     (rw, A["router_w"][0].rearrange("(c p) e -> p c e", p=P)),
                     (rb, A["router_b"][0:1, :].broadcast_to([P, E]))])
        PARAMS = len(params)

        slot_in = [sem(f"slot_in{i}") for i in range(SLOTS)]
        piece_done = sem("piece_done")
        x_in = [sem(f"x_in{t}") for t in range(NT)]
        x_again = sem("x_again")
        con_in = sem("con_in")
        rows_in = sem("rows_in")
        par_in = sem("par_in")
        bdown_in = sem("bdown_in")
        out_done = sem("out_done")
        dve_step = sem("dve_step")
        pool_step = sem("pool_step")
        cols_T = sem("cols_T")
        cols_ready = sem("cols_ready")
        x_sq = sem("x_sq")
        x_var = sem("x_var")
        x_std = sem("x_std")
        h_ready = sem("h_ready")
        h_T = sem("h_T")
        hT_ready = sem("hT_ready")
        strip_done = sem("strip_done")
        strip_free = [sem("strip_free0"), sem("strip_free1")]
        qk_var = sem("qk_var")
        qk_std = sem("qk_std")
        qk_ready = sem("qk_ready")
        qk_T = sem("qk_T")
        q_moved = sem("q_moved")
        k_moved = sem("k_moved")
        pooled = sem("pooled")
        scored = sem("scored")
        max_ready = sem("max_ready")
        exp_ready = sem("exp_ready")
        diff_ready = sem("diff_ready")
        diff_T = sem("diff_T")
        diffT_ready = sem("diffT_ready")
        o_done = sem("o_done")
        o_ready = sem("o_ready")
        o_var = sem("o_var")
        o_std = sem("o_std")
        o_normed = sem("o_normed")
        o_T = sem("o_T")
        oT_ready = sem("oT_ready")
        merged = sem("merged")
        wo_done = sem("wo_done")
        x2_ready = sem("x2_ready")
        x2_sq = sem("x2_sq")
        x2_var = sem("x2_var")
        x2_std = sem("x2_std")
        h2_ready = sem("h2_ready")
        h2_T = sem("h2_T")
        h2T_ready = sem("h2T_ready")
        logit_done = sem("logit_done")
        top_ready = sem("top_ready")
        top_exp = sem("top_exp")
        chosen_ready = sem("chosen_ready")
        comb_ready = sem("comb_ready")
        rank_done = sem("rank_done")
        comb_T = sem("comb_T")
        combT_ready = sem("combT_ready")
        lam_exp = sem("lam_exp")
        lam_sum = sem("lam_sum")
        rounds_ready = sem("rounds_ready")
        pick_ready = sem("pick_ready")
        gathered = sem("gathered")
        h_in_ready = sem("h_in_ready")
        g_ready = sem("g_ready")
        sig_ready = sem("sig_ready")
        act_ready = sem("act_ready")
        pick_T = sem("pick_T")
        pickT_ready = sem("pickT_ready")
        expert_step = sem("expert_step")
        hg_ready = sem("hg_ready")
        h_turned = sem("h_turned")
        act_T = sem("act_T")
        actT_ready = sem("actT_ready")
        y_ready = sem("y_ready")
        rows_zero = sem("rows_zero")
        bias_in = sem("bias_in")
        scattered = sem("scattered")
        out_ready = sem("out_ready")

        block = ctx.enter_context(nc.Block())

        w_in = A["w_in"][0].rearrange("(c p) n -> p c n", p=P)
        w_out = A["w_out"][0].rearrange("(c p) n -> p c n", p=P)

        def whole(w):
            return w.rearrange("(c p) n -> p c n", p=P)

        def cut(w, half):
            return w[:, :, HALF * half:HALF * (half + 1)]

        front = ([w_in[:, :, 512 + 512 * i:1024 + 512 * i] for i in range(3)] + [w_in[:, :, 0:512]]
                 + [w_in[:, :, 2048 + 512 * i:2560 + 512 * i] for i in range(2)]
                 + [whole(A["pool_up"][0])]
                 + [w_in[:, :, 3072 + 512 * i:3584 + 512 * i] for i in range(2)]
                 + [whole(A["attn_up"][0])] + [cut(w_out, 0), cut(w_out, 1)])
        Q_P, K_P, V_P, U_P, GA_P, PUP_P, GB_P, AUP_P, WO_P = 0, 1, 2, 3, 4, 6, 7, 9, 10
        FRONT = len(front)

        def slot(n, wide=False):
            if wide:
                return ring[:, n % SLOTS, :].rearrange("p (c n) -> p c n", c=4)
            return ring[:, n % SLOTS, :].rearrange("p (c n) -> p c n", c=NC)

        units = [(t, h) for t in range(NT) for h in range(HEADS)]
        STEPS_ATT = len(units) + 2
        strips = ([("qkv", i) for i in range(6)] + [("u", g) for g in range(NG)]
                  + [("gate", c) for c in range(NC)] + [("group", i) for i in range(2)]
                  + [("pup", c) for c in range(NC)] + [("gate", NC + c) for c in range(NC)]
                  + [("aup", c) for c in range(NC)])
        strip_no = {s: n for n, s in enumerate(strips)}

        def strip_bank(s):
            return ps[:, strip_no[s] % 2, :]

        def strip_wait(eng, s):
            eng.wait_ge(strip_done, strip_no[s] + 1)

        def strip_release(ins, s):
            ins.then_inc(strip_free[strip_no[s] % 2], 1)


        def strip_read(eng, s):
            eng.wait_ge(strip_free[strip_no[s] % 2], strip_no[s] // 2 + 1)

        def front_piece_free(eng, n):
            last = {Q_P: ("qkv", 1), K_P: ("qkv", 3), V_P: ("qkv", 5), U_P: ("u", 3), GA_P: ("gate", 3),
                    GA_P + 1: ("gate", 7), PUP_P: ("pup", NC - 1), GB_P: ("gate", 11), GB_P + 1: ("gate", 15),
                    AUP_P: ("aup", NC - 1)}
            if n in last:
                strip_wait(eng, last[n])
            else:
                eng.wait_ge(wo_done, NT)

        @block.sync
        def _(sp):
            for t in range(NT):
                sp.dma_start(xt[:, t, :], A["x"][0, P * t:P * (t + 1), :]).then_inc(x_in[t], 16)
            for n, src in enumerate(front):
                if n >= SLOTS:
                    front_piece_free(sp, n - SLOTS)
                sp.dma_start(slot(n, wide=src.shape[1] == 4), src).then_inc(slot_in[n % SLOTS], 16)
                if n == SLOTS:
                    sp.wait_ge(qk_T, 4)
                    for t in range(NT):
                        sp.dma_start(xt[:, t, :], A["x"][0, P * t:P * (t + 1), :]).then_inc(x_again, 16)

            def expert_pieces(step, at, first=False):
                for j in range(UNROLL):
                    for m, name in enumerate(("exp_w_gate", "exp_w_up", "exp_w_down")):
                        w = A[name][0].rearrange("e (c p) n -> p e c n", p=P)
                        for half in range(2):
                            n = PIECES_PER_EXPERT * j + 2 * m + half
                            if first and n < SLOTS:
                                front_piece_free(sp, FRONT - SLOTS + n)
                            else:
                                sp.wait_ge(piece_done, at * (UNROLL * PIECES_PER_EXPERT) + (n - SLOTS + 1))
                            src = w[:, bass.ds(step * UNROLL + j, 1), 4 * half:4 * half + 4, :]
                            src = src.rearrange("p e c n -> p (e c) n")
                            sp.dma_start(slot(FRONT + n, wide=True), src).then_inc(slot_in[(FRONT + n) % SLOTS], 16)

            expert_pieces(0, 0, first=True)
            with sp.Fori(1, STEPS) as step:
                expert_pieces(step, step)
            sp.wait_ge(rounds_ready, 1)
            rounds = sp.value_load(rounds_i[0:1, 0:1], min_val=1, max_val=ROUNDS)
            with sp.If(rounds > 1):
                with sp.Fori(1, rounds) as r:
                    with sp.Fori(0, STEPS) as step:
                        expert_pieces(step, r * STEPS + step)
            for t in range(NT):
                sp.wait_ge(out_ready, 2 * t + 2)
                sp.dma_start(out[0, P * t:P * (t + 1), :], xt[:, t, :]).then_inc(out_done, 16)
            sp.wait_ge(out_done, 16 * NT)

        @block.tensor
        def _(pe):
            mm, tr = nc.tensor.matmul, nc.tensor.transpose

            def piece_wait(n):
                pe.wait_ge(slot_in[n % SLOTS], 16 * (n // SLOTS + 1))

            def strip_start(s):
                n = strip_no[s]
                if n >= 2:
                    pe.wait_ge(strip_free[n % 2], n // 2)

            pe.wait_ge(con_in, 16)
            pe.wait_ge(rows_in, 16 * 5)
            tr(ps[:, 0, 0:R_ROWS], prow[0:R_ROWS, :], ident[0:R_ROWS, 0:R_ROWS]).then_inc(cols_T, 1)
            for t in range(NT):
                pe.wait_ge(h_ready, t + 1)
                for q in range(2):
                    for c in range(4):
                        last = tr(ps[:, 2 + 2 * t + q, P * c:P * (c + 1)],
                                  xt[:, t, P * (4 * q + c):P * (4 * q + c + 1)], ident)
                    last.then_inc(h_T, 1)

            pe.wait_ge(hT_ready, 4)
            pe.wait_ge(cols_ready, 1)
            for i, piece in enumerate((Q_P, K_P, V_P)):
                piece_wait(piece)
                for t in range(NT):
                    s = ("qkv", 2 * i + t)
                    strip_start(s)
                    for c in range(NC):
                        last = mm(strip_bank(s), hT[:, c, P * t:P * (t + 1)], slot(piece)[:, c, :],
                                  start=(c == 0), stop=(c == NC - 1))
                    last.then_inc(strip_done, 1)

            for w in range(2):
                pe.wait_ge(qk_ready, NT * (w + 1))
                for t in range(NT):
                    for h in range(HEADS):
                        last = tr(ps[:, 4 + 2 * w + t, P * h:P * (h + 1)], qk_tok[:, w, t, P * h:P * (h + 1)], ident)
                    last.then_inc(qk_T, 1)

            def by_channel(s, piece, cc):
                strip_start(s)
                for c in range(NC):
                    last = mm(strip_bank(s)[:, 0:S], slot(piece)[:, c, P * cc:P * (cc + 1)], hT[:, c, :],
                              start=(c == 0), stop=(c == NC - 1))
                last.then_inc(strip_done, 1)

            def u_strip(g):
                if g == 0:
                    piece_wait(U_P)
                by_channel(("u", g), U_P, g)

            def gate_strip(c):
                piece = (GA_P if c < NC else GB_P) + (c % NC) // 4
                if c % 4 == 0:
                    piece_wait(piece)
                by_channel(("gate", c), piece, c % 4)

            u_strip(0)
            u_strip(1)
            fill = [lambda: u_strip(2), lambda: u_strip(3)] + [lambda c=c: gate_strip(c) for c in range(NC)]

            for step in range(STEPS_ATT):
                if step < len(units):
                    t, h = units[step]
                    keys = P * (t + 1)
                    if step == 0:
                        pe.wait_ge(q_moved, 2)
                        pe.wait_ge(k_moved, 2)
                    if step >= 2:
                        pe.wait_ge(exp_ready, 2 * (step - 1))
                    for m in range(2):
                        b = 4 + 2 * (step % 2) + m
                        rows = slice(HD * m, HD * (m + 1))
                        mm(ps[:, b, 0:keys], qT[rows, h, P * t:P * (t + 1)], kT[rows, h, 0:keys],
                           start=True, stop=True)
                    for m in range(2):
                        b = 4 + 2 * (step % 2) + m
                        last = mm(ps[:, b, keys - CHUNK:keys], con[0:1, C_MASKQ:C_MASKQ + P],
                                  con[0:1, C_MASKK:C_MASKK + CHUNK], start=False, stop=True, skip_group_check=True)
                    last.then_inc(scored, 1)
                fill[step]()
                if 1 <= step <= len(units):
                    t, h = units[step - 1]
                    pe.wait_ge(diff_ready, step)
                    if step >= 2:
                        pe.wait_ge(diffT_ready, step - 1)
                    for kc in range(t + 1):
                        last = tr(ps[:, 2, P * kc:P * (kc + 1)], diff[:, (step - 1) % 2, P * kc:P * (kc + 1)], ident)
                    last.then_inc(diff_T, 1)
                if step >= 2:
                    t, h = units[step - 2]
                    pe.wait_ge(diffT_ready, step - 1)
                    if step == 2:
                        strip_read(pe, ("qkv", 4))
                        strip_read(pe, ("qkv", 5))
                    if step >= 3:
                        pe.wait_ge(o_ready, step - 2)
                    for kc in range(t + 1):
                        last = mm(ps[:, 3, 0:VD], diffT[:, step % 2, P * kc:P * (kc + 1)],
                                  vtok[:, kc, VD * h:VD * (h + 1)], start=(kc == 0), stop=(kc == t))
                    last.then_inc(o_done, 1)

            pe.wait_ge(par_in, 16 * PARAMS)
            pe.wait_ge(pooled, NG)
            for i in range(2):
                s = ("group", i)
                strip_start(s)
                for g in range(2):
                    last = mm(strip_bank(s)[:, S * g:S * (g + 1)], poolw[:, 2 * i + g, :], pT[:, 2 * i + g, :],
                              start=True, stop=True)
                last.then_inc(strip_done, 1)

            def up(kind, piece, src):
                piece_wait(piece)
                for m in range(NC):
                    strip_start((kind, m))
                    for k in range(4):
                        last = mm(strip_bank((kind, m))[:, 0:S], slot(piece, wide=True)[:, k, P * m:P * (m + 1)],
                                  src[:, k, :], start=(k == 0), stop=(k == 3))
                    last.then_inc(strip_done, 1)

            strip_read(pe, ("group", 0))
            strip_read(pe, ("group", 1))
            up("pup", PUP_P, yT)
            for c in range(NC, 2 * NC):
                gate_strip(c)

            for t in range(NT):
                pe.wait_ge(o_normed, t + 1)
                for h in range(HEADS):
                    last = tr(ps[:, 2 + t, P * h:P * (h + 1)], otok[:, t, VD * h:VD * (h + 1)], ident)
                last.then_inc(o_T, 1)
            pe.wait_ge(oT_ready, 2)
            up("aup", AUP_P, oT)

            piece_wait(WO_P)
            piece_wait(WO_P + 1)
            for t in range(NT):
                for m in range(NC):
                    if t == 0:
                        pe.wait_ge(merged, m + 1)
                    for half in range(2):
                        last = mm(ps[:, 4 + 2 * t + half, :], gate[:, m, P * t:P * (t + 1)],
                                  slot(WO_P + half)[:, m, :], start=(m == 0), stop=(m == NC - 1))
                last.then_inc(wo_done, 1)

            for t in range(NT):
                pe.wait_ge(h2_ready, t + 1)
                for q in range(2):
                    for c in range(4):
                        last = tr(ps[:, 2 * t + q, P * c:P * (c + 1)],
                                  h2[:, t, P * (4 * q + c):P * (4 * q + c + 1)], ident)
                    last.then_inc(h2_T, 1)
            for t in range(NT):
                pe.wait_ge(h2T_ready, 2 * t + 2)
                for c in range(NC):
                    last = mm(ps[:, 4 + 2 * t, 0:E], h2T[:, c, P * t:P * (t + 1)], rw[:, c, :],
                              start=(c == 0), stop=(c == NC - 1))
                last.then_inc(logit_done, 1)
            pe.wait_ge(chosen_ready, 1)
            mm(ps[:, 5, 0:E], tri, chosen[:, 0, :], start=True, stop=True).then_inc(rank_done, 1)
            pe.wait_ge(chosen_ready, 2)
            mm(ps[:, 7, 0:E], ones, chosen[:, 0, :], start=True, stop=False)
            mm(ps[:, 7, 0:E], tri, chosen[:, 1, :], start=False, stop=True).then_inc(rank_done, 1)
            for t in range(NT):
                last = mm(ps[0:1, 3, 0:E], ones[:, 0:1], chosen[:, t, :], start=(t == 0), stop=(t == NT - 1))
            last.then_inc(rank_done, 1)
            pe.wait_ge(comb_ready, 2)
            for t in range(NT):
                last = tr(ps[0:E, 2, P * t:P * (t + 1)], combf[:, t, :], ident)
            last.then_inc(comb_T, 1)
            pe.wait_ge(combT_ready, 1)
            pe.wait_ge(bdown_in, 16)
            pe.wait_ge(rounds_ready, 1)
            for t in range(NT):
                for half in range(2):
                    mm(ps[:, 2 * t + half, :], combT[0:E, P * t:P * (t + 1)], bdown[:, HALF * half:HALF * (half + 1)],
                       start=True, stop=True)

            def gather(buf):
                for t in range(NT):
                    for half in range(2):
                        last = mm(ps[BLOCK * half:BLOCK * (half + 1), 6, :], pick[:, buf, t, :],
                                  h2[:, t, HALF * half:HALF * (half + 1)], start=(t == 0), stop=(t == NT - 1))
                last.then_inc(gathered, 1)

            def turn(bank, src):
                for c in range(4):
                    last = tr(ps[:, bank, P * c:P * (c + 1)], src[:, P * c:P * (c + 1)], ident)
                return last

            def scatter():
                for t in range(NT):
                    for half in range(2):
                        rows = slice(BLOCK * half, BLOCK * (half + 1))
                        last = mm(ps[:, 2 * t + half, :], pickT[rows, P * t:P * (t + 1)], y_e[rows, :],
                                  start=False, stop=True, skip_group_check=True)
                return last

            pe.wait_ge(pick_ready, 1)
            gather(0)
            pe.wait_ge(hg_ready, 1)
            turn(6, h_got).then_inc(h_turned, 1)
            pe.wait_ge(rows_zero, 1)
            pe.wait_ge(bias_in, 32)

            rounds = pe.value_load(rounds_i[0:1, 0:1], min_val=1, max_val=ROUNDS)
            with pe.Fori(0, rounds) as r:
                with pe.Fori(0, STEPS) as step:
                    done = (r * STEPS + step) * UNROLL
                    landed = (r * STEPS + step) * (16 * UNROLL * PIECES_PER_EXPERT // SLOTS)
                    for j in range(UNROLL):
                        buf = j % 2

                        def product(k, bank, src, first):
                            n = FRONT + PIECES_PER_EXPERT * j + k
                            pe.wait_ge(slot_in[n % SLOTS], landed + 16 * (n // SLOTS + 1))
                            for c in range(4):
                                for half in range(2):
                                    last = mm(ps[BLOCK * half:BLOCK * (half + 1), bank, :], src[:, c, k % 2, :],
                                              slot(n, wide=True)[:, c, HALF * half:HALF * (half + 1)],
                                              start=(first and c == 0), stop=(k % 2 == 1 and c == 3))
                            last.then_inc(piece_done, 1)

                        def biases(k, bank):
                            for half in range(2):
                                mm(ps[BLOCK * half:BLOCK * (half + 1), bank, :], this_e[:, buf, k, :],
                                   bias_rows[:, HALF * half:HALF * (half + 1)], start=True, stop=False)

                        pe.wait_ge(h_in_ready, done + (j + 1))
                        biases(0, 4)
                        product(0, 4, h_in[:, buf], False)
                        product(1, 4, h_in[:, buf], False)
                        pe.wait_ge(pickT_ready, done + (j + 1))
                        biases(1, 5)
                        product(2, 5, h_in[:, buf], False)
                        product(3, 5, h_in[:, buf], False)
                        pe.wait_ge(y_ready, done + (j + 1))
                        scatter()
                        pe.wait_ge(pick_ready, done + (j + 2))
                        gather(1 - buf)
                        pe.wait_ge(act_ready, done + (j + 1))
                        turn(7, act_out).then_inc(act_T, 1)
                        pe.wait_ge(hg_ready, done + (j + 2))
                        turn(6, h_got).then_inc(h_turned, 1)
                        pe.wait_ge(actT_ready, done + (j + 1))
                        product(4, 7, actT, True)
                        product(5, 7, actT, False)
                        for t in range(NT):
                            last = tr(ps[:, 5, P * t:P * (t + 1)], pickw[:, buf, t].rearrange("p h s -> p (h s)"), ident)
                        last.then_inc(pick_T, 1)
            pe.wait_ge(pickT_ready, rounds * E + 1)
            pe.wait_ge(y_ready, rounds * E + 1)
            scatter().then_inc(scattered, 1)

        @block.scalar
        def _(act):
            fn = nc.scalar.activation
            act.dma_start(con[:], consts).then_inc(con_in, 16)
            for r0, src in ((R_MIXG, A["mix_norm_g"].rearrange("l (c p) -> (l c) p", p=P)),
                            (R_BGATE, A["b_branch_gate"].rearrange("l (c p) -> (l c) p", p=P)),
                            (R_PSCALE, A["pool_scale"].rearrange("l (c p) -> (l c) p", p=P)),
                            (R_SUBLN, A["subln_g"]),
                            (R_FFNG, A["ffn_norm_g"].rearrange("l (c p) -> (l c) p", p=P))):
                act.dma_start(prow[r0:r0 + src.shape[0], :], src).then_inc(rows_in, 16)
            for dst, src in params:
                act.dma_start(dst, src).then_inc(par_in, 16)

            for t in range(NT):
                act.wait_ge(x_in[t], 16)
                fn(junk[:, t, :], xt[:, t, :], ACT.Square, accum_out=ss[:, t:t + 1]).then_inc(x_sq, 1)
            for t in range(NT):
                act.wait_ge(x_var, t + 1)
                fn(rstd[:, t:t + 1], rstd[:, t:t + 1], ACT.Sqrt).then_inc(x_std, 1)

            for i in range(4):
                w, t = divmod(i, NT)
                s = ("qkv", i)
                strip_wait(act, s)
                if t == 0 and w == 0:
                    act.wait_ge(h_T, 4)
                nc.scalar.copy(qk_tok[:, w, t, :], strip_bank(s))
                if i >= 2:
                    act.wait_ge(qk_var, i - 1)
                strip_release(fn(squares[:, i % 2, :], strip_bank(s), ACT.Square), s)
                act.wait_ge(qk_var, i + 1)
                fn(qrs[:, i, :], qrs[:, i, :], ACT.Sqrt).then_inc(qk_std, 1)
            for t in range(NT):
                s = ("qkv", 4 + t)
                strip_wait(act, s)
                strip_release(nc.scalar.copy(vtok[:, t, :], strip_bank(s)), s)
            act.wait_ge(lam_sum, 1)
            fn(lam2, lam2, ACT.Exp).then_inc(lam_exp, 1)
            for t in range(NT):
                act.wait_ge(qk_T, t + 1)
                nc.scalar.copy(qT[:, :, P * t:P * (t + 1)],
                               ps[:, 4 + t, :].rearrange("p (h s) -> p h s", h=HEADS)).then_inc(q_moved, 1)

            def u_copy(g):
                s = ("u", g)
                strip_wait(act, s)
                strip_release(nc.scalar.copy(uT[:, g, PAD:], strip_bank(s)[:, 0:S]), s)

            def gate_e(c):
                s = ("gate", c)
                strip_wait(act, s)
                strip_release(fn(gate[:, c, :], strip_bank(s)[:, 0:S], ACT.Exp, bias=ngate[:, c:c + 1], scale=-1.0), s)

            u_copy(0)
            u_copy(1)
            fill = [lambda: u_copy(2), lambda: u_copy(3)] + [lambda c=c: gate_e(c) for c in range(NC)]
            for step in range(STEPS_ATT):
                b = step % 2
                if step < len(units):
                    t, h = units[step]
                    keys = P * (t + 1)
                    act.wait_ge(max_ready, step + 1)
                    for m in range(2):
                        fn(prob[:, b, m, 0:keys], ps[:, 4 + 2 * b + m, 0:keys], ACT.Exp, bias=mx[:, b, m:m + 1],
                           scale=HD ** -0.5, accum_out=den[:, b, m:m + 1]).then_inc(exp_ready, 1)
                fill[step]()
                if 1 <= step <= len(units):
                    t, h = units[step - 1]
                    act.wait_ge(diff_T, step)
                    nc.scalar.copy(diffT[:, (step - 1) % 2, 0:P * (t + 1)], ps[:, 2, 0:P * (t + 1)]).then_inc(diffT_ready, 1)
                if step >= 2:
                    t, h = units[step - 2]
                    act.wait_ge(o_done, step - 1)
                    nc.scalar.copy(otok[:, t, VD * h:VD * (h + 1)], ps[:, 3, 0:VD])
                    fn(junk_o[:], ps[:, 3, 0:VD], ACT.Square, accum_out=oss[:, step - 2:step - 1]).then_inc(o_ready, 1)
            for i in range(2):
                s = ("group", i)
                strip_wait(act, s)
                for g in range(2):
                    last = fn(yT[:, 2 * i + g, :], strip_bank(s)[:, S * g:S * (g + 1)], ACT.Copy,
                              scale=cols[:, R_PSCALE + 2 * i + g:R_PSCALE + 2 * i + g + 1])
                strip_release(last, s)
            act.wait_ge(o_var, 1)
            fn(ors, ors, ACT.Sqrt).then_inc(o_std, 1)
            for c in range(NC, 2 * NC):
                gate_e(c)
            for t in range(NT):
                act.wait_ge(o_T, t + 1)
                fn(oT[:, :, P * t:P * (t + 1)], ps[:, 2 + t, :].rearrange("p (h s) -> p h s", h=HEADS), ACT.Copy,
                   scale=subln8).then_inc(oT_ready, 1)

            for t in range(NT):
                act.wait_ge(x2_ready, 2 * t + 2)
                if t == 0:
                    act.dma_start(bdown, A["exp_b_down"][0]).then_inc(bdown_in, 16)
                    for k, name in enumerate(("exp_b_gate", "exp_b_up")):
                        act.dma_start(bias_rows[E * k:E * (k + 1), :], A[name][0]).then_inc(bias_in, 16)
                fn(junk[:, t, :], xt[:, t, :], ACT.Square, accum_out=ss[:, t:t + 1]).then_inc(x2_sq, 1)
                act.wait_ge(x2_var, t + 1)
                fn(rstd[:, t:t + 1], rstd[:, t:t + 1], ACT.Sqrt).then_inc(x2_std, 1)
            for t in range(NT):
                act.wait_ge(top_ready, t + 1)
                fn(topw[:, t, :], top[:, t, 0:TOPK], ACT.Exp, bias=nmax[:, t:t + 1],
                   accum_out=psum4[:, t:t + 1]).then_inc(top_exp, 1)
            act.wait_ge(comb_T, 1)
            nc.scalar.copy(combT[0:E, :], ps[0:E, 2, 0:S]).then_inc(combT_ready, 1)

            act.wait_ge(rounds_ready, 1)
            rounds = act.value_load(rounds_i[0:1, 0:1], min_val=1, max_val=ROUNDS)
            act.wait_ge(gathered, 1)
            nc.scalar.copy(h_got, ps[:, 6, :]).then_inc(hg_ready, 1)
            with act.Fori(0, rounds) as r:
                with act.Fori(0, STEPS) as step:
                    done = (r * STEPS + step) * UNROLL
                    for j in range(UNROLL):
                        act.wait_ge(g_ready, done + (j + 1))
                        fn(sig, g1, ACT.Sigmoid, scale=ALPHA).then_inc(sig_ready, 1)
                        act.wait_ge(gathered, done + (j + 2))
                        nc.scalar.copy(h_got, ps[:, 6, :]).then_inc(hg_ready, 1)
                        act.wait_ge(act_T, done + (j + 1))
                        nc.scalar.copy(actT.rearrange("p c h s -> p (c h s)"), ps[:, 7, :]).then_inc(actT_ready, 1)
                        act.wait_ge(piece_done, done * PIECES_PER_EXPERT + (PIECES_PER_EXPERT * j + 6))
                        nc.scalar.copy(y_e, ps[:, 7, :]).then_inc(y_ready, 1)
                        act.wait_ge(pick_T, done + (j + 1))
                        nc.scalar.copy(pickT, ps[:, 5, 0:S]).then_inc(pickT_ready, 1)

        @block.gpsimd
        def _(pool):
            steps = [0]

            def own(ins):
                steps[0] += 1
                ins.then_inc(pool_step, 1)
                pool.wait_ge(pool_step, steps[0])

            gp = nc.gpsimd
            own(gp.memset(uT[:, :, 0:PAD], 0.0))
            pool.wait_ge(con_in, 16)
            for g in range(NG):
                strip_read(pool, ("u", g))
                cur = uT[:, g, :]
                for k in range(g + 1):
                    lo, shift = (2 << k) - 1, 1 << k
                    nxt = sums[:, k % 2, :]
                    own(gp.tensor_tensor(nxt[:, lo:], cur[:, lo:], cur[:, lo - shift:S + PAD - shift], ALU.add))
                    cur = nxt
                gp.tensor_scalar(pT[:, g, 16:], cur[:, PAD + 16:], 1.0 / (2 << g), None, ALU.mult)
                own(gp.tensor_tensor(pT[:, g, 0:16], cur[:, PAD:PAD + 16], con[:, C_INV + 16 * g:C_INV + 16 * g + 16],
                                     ALU.mult))
                gp.tensor_tensor(pT[:, g, :], pT[:, g, :], uT[:, g, PAD:], ALU.subtract).then_inc(pooled, 1)
            pool.wait_ge(wo_done, NT)
            gp.memset(bias_rows[2 * E:, :], 0.0).then_inc(rows_zero, 1)

        @block.vector
        def _(dve):
            v = nc.vector
            steps = [0]

            def own(ins):
                steps[0] += 1
                ins.then_inc(dve_step, 1)
                dve.wait_ge(dve_step, steps[0])

            def wide(col, shape, axis):
                return col.unsqueeze(axis).broadcast_to(shape)

            for t in range(NT):
                dve.wait_ge(x_sq, t + 1)
                v.tensor_scalar(rstd[:, t:t + 1], ss[:, t:t + 1], 1.0 / D, EPS, ALU.mult, ALU.add).then_inc(x_var, 1)
            for t in range(NT):
                dve.wait_ge(x_std, t + 1)
                own(v.reciprocal(rstd[:, t:t + 1], rstd[:, t:t + 1]))
                v.tensor_scalar(xt[:, t, :], xt[:, t, :], rstd[:, t:t + 1], None, ALU.mult).then_inc(h_ready, 1)
            dve.wait_ge(cols_T, 1)
            v.tensor_copy(cols[:], ps[:, 0, 0:R_ROWS]).then_inc(cols_ready, 1)
            dve.wait_ge(cols_ready, 1)
            v.tensor_scalar(ngate, cols[:, R_BGATE:R_BGATE + 2 * NC], -1.0, None, ALU.mult)
            own(v.tensor_scalar(subln8, cols[:, R_SUBLN:R_SUBLN + 1], 1.0 - LAM_INIT, None, ALU.mult))
            for t in range(NT):
                for q in range(2):
                    dve.wait_ge(h_T, 2 * t + q + 1)
                    v.tensor_tensor(hT[:, 4 * q:4 * q + 4, P * t:P * (t + 1)],
                                    ps[:, 2 + 2 * t + q, :].rearrange("p (c s) -> p c s", c=4),
                                    wide(cols[:, R_MIXG + 4 * q:R_MIXG + 4 * q + 4], [P, 4, P], 2),
                                    ALU.mult).then_inc(hT_ready, 1)
            dve.wait_ge(par_in, 16 * PARAMS)
            own(v.tensor_tensor(lamv[:, 0:2, :], lamv[:, 0:2, :], lamv[:, 2:4, :], ALU.mult))
            v.tensor_reduce(lam2, lamv[:, 0:2, :], AX.X, ALU.add).then_inc(lam_sum, 1)

            for i in range(4):
                w, t = divmod(i, NT)
                strip_read(dve, ("qkv", i))
                own(v.tensor_reduce(qss[:, i, :], squares[:, i % 2, :].rearrange("p (g d) -> p g d", d=HD), AX.X, ALU.add))
                v.tensor_scalar(qrs[:, i, :], qss[:, i, :], 1.0 / HD, EPS, ALU.mult, ALU.add).then_inc(qk_var, 1)
                dve.wait_ge(qk_std, i + 1)
                own(v.reciprocal(qrs[:, i, :], qrs[:, i, :]))
                z = qk_tok[:, w, t, :].rearrange("p (g d) -> p g d", d=HD)
                own(v.tensor_tensor(z, z, wide(qrs[:, i, :], [P, 8, HD], 2), ALU.mult))
                own(v.tensor_tensor(z, z, wide((gq, gk)[w], [P, 8, HD], 1), ALU.mult))
                cosb = wide(con[:, C_COS + 8 * t:C_COS + 8 * t + 8], [P, 8, 8], 1)
                sinb = wide(con[:, C_SIN + 8 * t:C_SIN + 8 * t + 8], [P, 8, 8], 1)
                v.tensor_tensor(ropeb[:, :, 0:8], z[:, :, 8:16], sinb, ALU.mult)
                own(v.tensor_tensor(ropeb[:, :, 8:16], z[:, :, 0:8], sinb, ALU.mult))
                v.tensor_tensor(z[:, :, 0:8], z[:, :, 0:8], cosb, ALU.mult)
                own(v.tensor_tensor(z[:, :, 8:16], z[:, :, 8:16], cosb, ALU.mult))
                own(v.tensor_tensor(z[:, :, 0:8], z[:, :, 0:8], ropeb[:, :, 0:8], ALU.subtract))
                v.tensor_tensor(z[:, :, 8:16], z[:, :, 8:16], ropeb[:, :, 8:16], ALU.add).then_inc(qk_ready, 1)
            for t in range(NT):
                dve.wait_ge(qk_T, NT + t + 1)
                v.tensor_copy(kT[:, :, P * t:P * (t + 1)],
                              ps[:, 6 + t, :].rearrange("p (h s) -> p h s", h=HEADS)).then_inc(k_moved, 1)
            dve.wait_ge(lam_exp, 1)
            own(v.tensor_tensor(neglam, lam2[:, 1:2], lam2[:, 0:1], ALU.subtract))
            own(v.tensor_scalar(neglam, neglam, -LAM_INIT, None, ALU.add))

            def sigmoid_rest(c):
                strip_read(dve, ("gate", c))
                own(v.tensor_scalar(gate[:, c, :], gate[:, c, :], 1.0, None, ALU.add))
                return v.reciprocal(gate[:, c, :], gate[:, c, :])

            for step in range(len(units)):
                t, h = units[step]
                b, keys = step % 2, P * (t + 1)
                dve.wait_ge(scored, step + 1)
                own(v.tensor_reduce(mx[:, b, :], ps[:, 4 + 2 * b:6 + 2 * b, 0:keys], AX.X, ALU.max))
                v.tensor_scalar(mx[:, b, :], mx[:, b, :], -HD ** -0.5, None, ALU.mult).then_inc(max_ready, 1)
                dve.wait_ge(exp_ready, 2 * step + 2)
                own(v.reciprocal(den[:, b, :], den[:, b, :]))
                own(v.tensor_tensor(den[:, b, 1:2], den[:, b, 1:2], neglam, ALU.mult))
                own(v.tensor_scalar(prob[:, b, 1, 0:keys], prob[:, b, 1, 0:keys], den[:, b, 1:2], None, ALU.mult))
                v.scalar_tensor_tensor(out=diff[:, b, 0:keys], in0=prob[:, b, 0, 0:keys], scalar=den[:, b, 0:1],
                                       in1=prob[:, b, 1, 0:keys], op0=ALU.mult, op1=ALU.add).then_inc(diff_ready, 1)
                if step >= 2:
                    own(sigmoid_rest(step - 2))
            for c in range(len(units) - 2, NC):
                own(sigmoid_rest(c))

            dve.wait_ge(o_ready, len(units))
            v.tensor_scalar(ors, oss, 1.0 / VD, EPS, ALU.mult, ALU.add).then_inc(o_var, 1)
            dve.wait_ge(o_std, 1)
            own(v.reciprocal(ors, ors))
            for t in range(NT):
                z = otok[:, t, :].rearrange("p (h d) -> p h d", h=HEADS)
                v.tensor_tensor(z, z, wide(ors[:, HEADS * t:HEADS * (t + 1)], [P, HEADS, VD], 2),
                                ALU.mult).then_inc(o_normed, 1)
            for m in range(NC):
                s = ("pup", m)
                strip_wait(dve, s)
                strip_release(v.tensor_tensor(gate[:, m, :], strip_bank(s)[:, 0:S], gate[:, m, :], ALU.mult), s)
            for c in range(NC, 2 * NC):
                own(sigmoid_rest(c))
            for m in range(NC):
                s = ("aup", m)
                strip_wait(dve, s)
                strip_release(v.tensor_tensor(gate[:, NC + m, :], strip_bank(s)[:, 0:S], gate[:, NC + m, :], ALU.mult), s)
                strip_read(dve, s)
                v.tensor_tensor(gate[:, m, :], gate[:, m, :], gate[:, NC + m, :], ALU.add).then_inc(merged, 1)

            dve.wait_ge(x_again, 16 * NT)

            def residual(t):
                dve.wait_ge(wo_done, t + 1)
                for half in range(2):
                    z = xt[:, t, HALF * half:HALF * (half + 1)]
                    v.tensor_tensor(z, z, ps[:, 4 + 2 * t + half, :], ALU.add).then_inc(x2_ready, 1)
                dve.wait_ge(x2_sq, t + 1)
                v.tensor_scalar(rstd[:, t:t + 1], ss[:, t:t + 1], 1.0 / D, EPS, ALU.mult, ALU.add).then_inc(x2_var, 1)

            def normed(t):
                dve.wait_ge(x2_std, t + 1)
                own(v.reciprocal(rstd[:, t:t + 1], rstd[:, t:t + 1]))
                v.tensor_scalar(h2[:, t, :], xt[:, t, :], rstd[:, t:t + 1], None, ALU.mult).then_inc(h2_ready, 1)

            def turned(t, q):
                dve.wait_ge(h2_T, 2 * t + q + 1)
                v.tensor_tensor(h2T[:, 4 * q:4 * q + 4, P * t:P * (t + 1)],
                                ps[:, 2 * t + q, :].rearrange("p (c s) -> p c s", c=4),
                                wide(cols[:, R_FFNG + 4 * q:R_FFNG + 4 * q + 4], [P, 4, P], 2),
                                ALU.mult).then_inc(h2T_ready, 1)

            residual(0)
            normed(0)
            residual(1)
            turned(0, 0)
            normed(1)
            turned(0, 1)
            turned(1, 0)
            turned(1, 1)

            for t in range(NT):
                dve.wait_ge(logit_done, t + 1)
                own(v.tensor_tensor(logit[:, t, :], ps[:, 4 + 2 * t, 0:E], rb, ALU.add))
                own(v.max(top[:, t, :], logit[:, t, :]))
                v.tensor_scalar(nmax[:, t:t + 1], top[:, t, 0:1], -1.0, None, ALU.mult).then_inc(top_ready, 1)
                own(v.max_index(topi[:, t, :], top[:, t, :], logit[:, t, :]))
                own(v.tensor_copy(topf[:, t, :], topi[:, t, :]))
                own(v.tensor_tensor(eq4, wide(iota[:, 0:E], [P, TOPK, E], 1), wide(topf[:, t, 0:TOPK], [P, TOPK, E], 2),
                                    ALU.is_equal))
                v.tensor_reduce(chosen[:, t, :], eq4.rearrange("p k e -> p e k"), AX.X, ALU.add).then_inc(chosen_ready, 1)
                dve.wait_ge(top_exp, t + 1)
                own(v.reciprocal(psum4[:, t:t + 1], psum4[:, t:t + 1]))
                own(v.tensor_scalar(topw[:, t, :], topw[:, t, :], psum4[:, t:t + 1], None, ALU.mult))
                own(v.tensor_tensor(eq4w, eq4, wide(topw[:, t, :], [P, TOPK, E], 2), ALU.mult))
                v.tensor_reduce(combf[:, t, :], eq4w.rearrange("p k e -> p e k"), AX.X, ALU.add).then_inc(comb_ready, 1)
                dve.wait_ge(comb_ready, t + 1)
                v.tensor_copy(comb_tab[:, t, :].rearrange("p (r e) -> p r e", e=E),
                              wide(combf[:, t, :], [P, ROUNDS + 1, E], 1))
            for t in range(NT):
                dve.wait_ge(rank_done, t + 1)
                dve.wait_ge(chosen_ready, t + 1)
                own(v.tensor_tensor(ranks[:, t, :], ps[:, 5 + 2 * t, 0:E], chosen[:, t, :], ALU.mult))
                for r in range(ROUNDS + 1):
                    last = v.tensor_scalar(rank_tab[:, t, E * r:E * (r + 1)], ranks[:, t, :], -1.0 - BLOCK * r, None,
                                           ALU.add)
            own(last)

            def select(n, e, buf):
                for t in range(NT):
                    v.tensor_scalar(pick[:, buf, t, :], iota, rank_tab[:, t, bass.ds(n, 1)], None, ALU.is_equal)
                for t in range(NT):
                    v.tensor_scalar(pickw[:, buf, t], wide(iota, [P, 2, BLOCK], 1), rank_tab[:, t, bass.ds(n, 1)],
                                    comb_tab[:, t, bass.ds(n, 1)], ALU.is_equal, ALU.mult)
                for k in range(2):
                    last = v.tensor_copy(this_e[:, buf, k, :],
                                         con[:, bass.ds(e + (C_IDENT + E * k), 1)].broadcast_to([P, BLOCK]))
                last.then_inc(pick_ready, 1)

            v.memset(y_e, 0.0).then_inc(y_ready, 1)
            v.memset(pickT, 0.0).then_inc(pickT_ready, 1)
            select(0, 0, 0)
            dve.wait_ge(rank_done, 3)
            own(v.tensor_reduce(cnt, ps[0:1, 3, 0:E], AX.X, ALU.max))
            own(v.tensor_scalar(cnt2[:, 0:1], cnt, float(BLOCK), 1.0, ALU.is_gt, ALU.add))
            own(v.scalar_tensor_tensor(out=cnt2[:, 1:2], in0=cnt, scalar=2.0 * BLOCK, in1=cnt2[:, 0:1],
                                       op0=ALU.is_gt, op1=ALU.add))
            v.scalar_tensor_tensor(out=rounds_i[:], in0=cnt, scalar=3.0 * BLOCK, in1=cnt2[:, 1:2],
                                   op0=ALU.is_gt, op1=ALU.add).then_inc(rounds_ready, 1)

            def gathered_in(buf):
                gain = cols[:, R_FFNG:R_FFNG + NC].rearrange("p (h c) -> p c h", h=2)
                v.tensor_tensor(h_in[:, buf], ps[:, 6, :].rearrange("p (c h s) -> p c h s", c=4, h=2),
                                wide(gain, [P, 4, 2, BLOCK], 3), ALU.mult).then_inc(h_in_ready, 1)

            dve.wait_ge(h_turned, 1)
            gathered_in(0)

            dve.wait_ge(rounds_ready, 1)
            rounds = dve.value_load(rounds_i[0:1, 0:1], min_val=1, max_val=ROUNDS)
            with dve.Fori(0, rounds) as r:
                with dve.Fori(0, STEPS) as step:
                    done = (r * STEPS + step) * UNROLL
                    after = ((step + 1) & (STEPS - 1)) * UNROLL
                    for j in range(UNROLL):
                        dve.wait_ge(piece_done, done * PIECES_PER_EXPERT + (PIECES_PER_EXPERT * j + 2))
                        v.tensor_scalar(g1, ps[:, 4, :], LIMIT, None, ALU.min).then_inc(g_ready, 1)
                        e = (step * UNROLL + (j + 1)) if j < UNROLL - 1 else after
                        select(done + (j + 1), e, 1 - j % 2)
                        dve.wait_ge(sig_ready, done + (j + 1))
                        v.tensor_tensor(gs, g1, sig, ALU.mult).then_inc(expert_step, 1)
                        dve.wait_ge(piece_done, done * PIECES_PER_EXPERT + (PIECES_PER_EXPERT * j + 4))
                        v.tensor_scalar(u1, ps[:, 5, :], LIMIT, -LIMIT, ALU.min, ALU.max).then_inc(expert_step, 1)
                        dve.wait_ge(expert_step, done * 2 + (2 * j + 2))
                        v.scalar_tensor_tensor(out=act_out, in0=u1, scalar=1.0, in1=gs, op0=ALU.add,
                                               op1=ALU.mult).then_inc(act_ready, 1)
                        dve.wait_ge(h_turned, done + (j + 2))
                        gathered_in(1 - j % 2)
            dve.wait_ge(scattered, 1)
            for t in range(NT):
                for half in range(2):
                    z = xt[:, t, HALF * half:HALF * (half + 1)]
                    v.tensor_tensor(z, z, ps[:, 2 * t + half, :], ALU.add).then_inc(out_ready, 1)


_INS = ["x", "mix_norm_g", "w_in", "b_branch_gate", "pool_w", "pool_scale", "pool_up", "q_norm_g", "k_norm_g",
        "lambda_q1", "lambda_k1", "lambda_q2", "lambda_k2", "subln_g", "attn_up", "w_out", "ffn_norm_g",
        "router_w", "router_b", "exp_w_gate", "exp_b_gate", "exp_w_up", "exp_b_up", "exp_w_down", "exp_b_down"]


def kernel(**inputs):
    import concourse.bacc as _bacc
    from concourse.bass_utils import run_bass_kernel_spmd as _run

    nc = _bacc.Bacc("TRN2", target_bir_lowering=False, num_devices=1)
    arrays, aps = {}, {}
    for name in _INS:
        a = np.ascontiguousarray(inputs[name])
        arrays["in_" + name] = a
        aps[name] = nc.dram_tensor("in_" + name, a.shape, mybir.dt.from_np(a.dtype), kind="ExternalInput").ap()
    arrays["shape_constants"] = shape_constants()
    consts = nc.dram_tensor("shape_constants", (P, C_WIDTH), F32, kind="ExternalInput").ap()
    out = nc.dram_tensor("out", (1, S, D), F32, kind="ExternalOutput").ap()
    build(nc, aps, consts, out)
    r = _run(nc, [arrays], core_ids=[0])
    return r.results[0]["out"]
```

```python
from contextlib import ExitStack

import numpy as np

import concourse.bass as bass
from concourse import mybir

ALU = mybir.AluOpType
ACT = mybir.ActivationFunctionType
AX = mybir.AxisListType
F32 = mybir.dt.float32
BF16 = mybir.dt.bfloat16
I32 = mybir.dt.int32
U32 = mybir.dt.uint32

P = 128
D = 1024
S = 256
NT = S // P
NC = D // P
HEADS, HD, VD = 4, 64, 128
QK = HEADS * 2 * HD
POOLW = 512
NG = 4
PAD = 16
CHUNK = 64
ROT = HD // 4
E = 32
TOPK = 4
F = 1024
EPS = 1e-6
LIMIT, ALPHA = 7.0, 1.702
LAM_INIT = 0.8 - 0.6
MASKED = -1e30

HALF = 512
SLOTS = 8
PIECE = NC * HALF
BLOCK = 64
ROUNDS = S // BLOCK
UNROLL = 4
STEPS = E // UNROLL
PIECES_PER_EXPERT = 6

C_IDENT, C_TRI, C_ONES, C_IOTA, C_INV, C_COS, C_SIN, C_WIDTH = 0, 128, 256, 384, 448, 512, 528, 544
R_MIXG, R_BGATE, R_PSCALE, R_SUBLN, R_FFNG, R_ROWS = 0, 8, 24, 28, 29, 37


def shape_constants():
    c = np.zeros((P, C_WIDTH), np.float32)
    c[:, C_IDENT:C_IDENT + P] = np.eye(P)
    c[:, C_TRI:C_TRI + P] = np.triu(np.ones((P, P)))
    c[:, C_ONES:C_ONES + P] = 1.0
    c[:, C_IOTA:C_IOTA + BLOCK] = np.arange(BLOCK)
    for g in range(NG):
        c[:, C_INV + 16 * g:C_INV + 16 * (g + 1)] = 1.0 / np.minimum(np.arange(1, 17), 2 << g)
    inv = (np.float32(500000.0) ** (-np.arange(0, ROT, 2, dtype=np.float32) / np.float32(ROT))).astype(np.float32)
    ang = np.arange(S, dtype=np.float32)[:, None] * inv[None, :]
    for t in range(NT):
        c[:, C_COS + 8 * t:C_COS + 8 * t + 8] = np.cos(ang[P * t:P * (t + 1)])
        c[:, C_SIN + 8 * t:C_SIN + 8 * t + 8] = np.sin(ang[P * t:P * (t + 1)])
    return c


def build(nc, A, consts, out):
    with ExitStack() as ctx:
        def sb(name, shape, dt=F32):
            return ctx.enter_context(nc.sbuf_tensor(name, shape, dt))

        def sem(name):
            return ctx.enter_context(nc.semaphore(name))

        ps = ctx.enter_context(nc.psum_tensor("ps", [P, 8, HALF], F32))

        ring = sb("ring", [P, SLOTS, PIECE])
        xt = sb("xt", [P, NT, D])
        qk_tok = xt[:].rearrange("p t (w c) -> p w t c", w=2)
        con = sb("con", [P, C_WIDTH])
        cols = sb("cols", [P, R_ROWS])
        small = sb("small", [P, 256])
        arena = sb("arena", [P, 16400])
        ident = con[:, C_IDENT:C_IDENT + P]
        tri = con[:, C_TRI:C_TRI + P]
        ones = con[:, C_ONES:C_ONES + P]
        iota = con[:, C_IOTA:C_IOTA + BLOCK]

        taken = [0]

        def part(n):
            at = taken[0]
            taken[0] += n
            assert taken[0] <= 16400, taken[0]
            return arena[:, at:at + n]

        hT = part(NC * S).rearrange("p (c s) -> p c s", c=NC)
        qT = part(HEADS * S).rearrange("p (h s) -> p h s", h=HEADS)
        kT = part(HEADS * S).rearrange("p (h s) -> p h s", h=HEADS)
        gate = part(2 * NC * S).rearrange("p (c s) -> p c s", c=2 * NC)
        vtok = part(NT * 512).rearrange("p (t c) -> p t c", t=NT)
        uT = part(NG * (S + PAD)).rearrange("p (g s) -> p g s", g=NG)
        pT = part(NG * S).rearrange("p (g s) -> p g s", g=NG)
        sums = part(2 * (S + PAD)).rearrange("p (b s) -> p b s", b=2)
        prob = part(2 * 2 * S).rearrange("p (b m s) -> p b m s", b=2, m=2)
        diff = part(2 * S).rearrange("p (b s) -> p b s", b=2)
        diffT = part(2 * S).rearrange("p (b s) -> p b s", b=2)
        otok_flat = part(NT * 512)
        otok = otok_flat.rearrange("p (t c) -> p t c", t=NT)
        oT = qT
        yT = uT[:, :, PAD:]
        prow = otok_flat[:, 0:P]
        lamv = otok_flat[:, P:P + 4 * HD].rearrange("p (i d) -> p i d", i=4)
        squares = prob.rearrange("p b m s -> p b (m s)")
        junk = gate[:, NC:, :].rearrange("p (t c) s -> p t (c s)", t=NT)
        first_end = taken[0]
        gq = part(HD)
        gk = part(HD)
        poolw = part(NG * P).rearrange("p (g d) -> p g d", g=NG)
        rw = part(NC * E).rearrange("p (c e) -> p c e", c=NC)
        rb = part(E)
        h2 = hT.rearrange("p c s -> p (c s)").rearrange("p (t d) -> p t d", t=NT)
        taken[0] = NC * S
        h2T = part(NC * S).rearrange("p (c s) -> p c s", c=NC)
        h_in = part(2 * NC * BLOCK).rearrange("p (b c h s) -> p b c h s", b=2, c=4, h=2)
        h_got = part(HALF)
        g1 = part(HALF)
        sig = part(HALF)
        gs = part(HALF)
        u1 = part(HALF)
        act_out = part(HALF)
        actT = part(NC * BLOCK).rearrange("p (c h s) -> p c h s", c=4, h=2)
        y_e = part(HALF)
        pickT = part(S)
        pick = part(2 * NT * BLOCK).rearrange("p (b t s) -> p b t s", b=2, t=NT)
        pickw = part(2 * NT * 2 * BLOCK).rearrange("p (b t h s) -> p b t h s", b=2, t=NT, h=2)
        this_e = part(2 * 3 * BLOCK).rearrange("p (b k s) -> p b k s", b=2, k=3)
        bias_rows = part(D)
        rank_tab = part(NT * (ROUNDS + 1) * E).rearrange("p (t n) -> p t n", t=NT)
        comb_tab = part(NT * (ROUNDS + 1) * E).rearrange("p (t n) -> p t n", t=NT)
        eq4 = part(NT * TOPK * E).rearrange("p (t k e) -> p t k e", t=NT, k=TOPK)
        eq4w = part(NT * TOPK * E).rearrange("p (t k e) -> p t k e", t=NT, k=TOPK)
        logit = part(NT * E).rearrange("p (t e) -> p t e", t=NT)
        chosen = part(NT * E).rearrange("p (t e) -> p t e", t=NT)
        combf = part(NT * E).rearrange("p (t e) -> p t e", t=NT)
        ranks = part(NT * E).rearrange("p (t e) -> p t e", t=NT)
        logitT = g1[:, 0:S]
        assert taken[0] <= first_end, (taken[0], first_end)
        top = sb("top", [P, NT, 8])
        topi = sb("topi", [P, NT, 8], U32)
        topf = sb("topf", [P, NT, 8])
        topw = sb("topw", [P, NT, TOPK])
        junk_o = sb("junk_o", [P, VD])
        scrap = sb("scrap", [P, 2])
        mask_q = sb("mask_q", [1, P], BF16)
        mask_k = sb("mask_k", [1, CHUNK], BF16)
        zrow = sb("zrow", [1, HALF], BF16)
        rounds_i = sb("rounds_i", [1, 1], I32)

        ss = small[:, 0:2]
        rstd = small[:, 2:4]
        qss = small[:, 8:40].rearrange("p (i g) -> p i g", i=4)
        qrs = small[:, 40:72].rearrange("p (i g) -> p i g", i=4)
        lam2 = small[:, 136:138]
        neglam = small[:, 138:139]
        mx = small[:, 140:144].rearrange("p (b m) -> p b m", b=2)
        den = small[:, 144:148].rearrange("p (b m) -> p b m", b=2)
        oss = small[:, 152:160]
        ors = small[:, 160:168]
        ngate = small[:, 168:184]
        subln8 = small[:, 184:185]
        psum4 = small[:, 188:190]
        ss2 = small[:, 196:200].rearrange("p (t h) -> p t h", t=NT)
        cnt = small[0:1, 192:193]
        cnt2 = small[0:1, 194:196]
        ropeb = sb("ropeb", [P, 8, 16])

        params = ([(gq, A["q_norm_g"][0:1, :].broadcast_to([P, A["q_norm_g"].shape[1]])), (gk, A["k_norm_g"][0:1, :].broadcast_to([P, A["k_norm_g"].shape[1]]))]
                  + [(lamv[:, i, :], A[n][0:1, :].broadcast_to([P, HD]))
                     for i, n in enumerate(("lambda_q1", "lambda_q2", "lambda_k1", "lambda_k2"))]
                  + [(poolw, A["pool_w"][0].rearrange("g c d -> c g d")),
                     (rw, A["router_w"][0].rearrange("(c p) e -> p c e", p=P)),
                     (rb, A["router_b"][0:1, :].broadcast_to([P, E]))])
        rows = [(R_MIXG, A["mix_norm_g"].rearrange("l (c p) -> (l c) p", p=P)),
                (R_BGATE, A["b_branch_gate"].rearrange("l (c p) -> (l c) p", p=P)),
                (R_PSCALE, A["pool_scale"].rearrange("l (c p) -> (l c) p", p=P)),
                (R_SUBLN, A["subln_g"]),
                (R_FFNG, A["ffn_norm_g"].rearrange("l (c p) -> (l c) p", p=P))]
        PARAMS = len(params)

        slot_in = [sem(f"slot_in{i}") for i in range(SLOTS)]
        piece_done = sem("piece_done")
        zero_col = sem("zero_col")
        x_in = [sem(f"x_in{t}") for t in range(NT)]
        x_again = sem("x_again")
        con_in = sem("con_in")
        rows_in = sem("rows_in")
        par_in = sem("par_in")
        out_done = sem("out_done")
        dve_step = sem("dve_step")
        pool_step = sem("pool_step")
        cols_T = sem("cols_T")
        cols_ready = sem("cols_ready")
        x_sq = sem("x_sq")
        x_var = sem("x_var")
        x_std = sem("x_std")
        h_ready = sem("h_ready")
        h_T = sem("h_T")
        hT_ready = sem("hT_ready")
        strip_done = sem("strip_done")
        strip_free = [sem("strip_free0"), sem("strip_free1")]
        qk_var = sem("qk_var")
        qk_std = sem("qk_std")
        qk_ready = sem("qk_ready")
        qk_T = sem("qk_T")
        q_moved = sem("q_moved")
        k_moved = sem("k_moved")
        pooled = sem("pooled")
        scored = sem("scored")
        max_ready = sem("max_ready")
        exp_ready = sem("exp_ready")
        diff_ready = sem("diff_ready")
        diff_T = sem("diff_T")
        diffT_ready = sem("diffT_ready")
        o_done = sem("o_done")
        o_ready = sem("o_ready")
        o_var = sem("o_var")
        o_std = sem("o_std")
        o_normed = sem("o_normed")
        o_T = sem("o_T")
        oT_ready = sem("oT_ready")
        merged = sem("merged")
        wo_done = sem("wo_done")
        x2_ready = sem("x2_ready")
        x2_sq = sem("x2_sq")
        x2_var = sem("x2_var")
        x2_std = sem("x2_std")
        h2_ready = sem("h2_ready")
        h2_T = sem("h2_T")
        logit_done = sem("logit_done")
        top_ready = sem("top_ready")
        top_exp = sem("top_exp")
        rw_ready = sem("rw_ready")
        h2T_even = sem("h2T_even")
        h2T_odd = sem("h2T_odd")
        logitT_ready = sem("logitT_ready")
        logit_T = sem("logit_T")
        zero_row = sem("zero_row")
        mask_ready = sem("mask_ready")
        chosen_ready = sem("chosen_ready")
        rank_done = sem("rank_done")
        lam_exp = sem("lam_exp")
        lam_sum = sem("lam_sum")
        rounds_ready = sem("rounds_ready")
        pick_ready = sem("pick_ready")
        gathered = sem("gathered")
        h_in_ready = sem("h_in_ready")
        g_ready = sem("g_ready")
        sig_ready = sem("sig_ready")
        act_ready = sem("act_ready")
        pick_T = sem("pick_T")
        pickT_ready = sem("pickT_ready")
        expert_step = sem("expert_step")
        hg_ready = sem("hg_ready")
        h_turned = sem("h_turned")
        act_T = sem("act_T")
        actT_ready = sem("actT_ready")
        y_ready = sem("y_ready")
        rows_zero = sem("rows_zero")
        bias_in = sem("bias_in")
        scattered = sem("scattered")
        out_ready = sem("out_ready")

        block = ctx.enter_context(nc.Block())

        w_in = A["w_in"][0].rearrange("(c p) n -> p c n", p=P)
        w_out = A["w_out"][0].rearrange("(c p) n -> p c n", p=P)

        def whole(w):
            return w.rearrange("(c p) n -> p c n", p=P)

        def cut(w, half):
            return w[:, :, HALF * half:HALF * (half + 1)]

        front = ([w_in[:, :, 512 + 512 * i:1024 + 512 * i] for i in range(3)] + [w_in[:, :, 0:512]]
                 + [w_in[:, :, 2048 + 512 * i:2560 + 512 * i] for i in range(2)]
                 + [whole(A["pool_up"][0])]
                 + [w_in[:, :, 3072 + 512 * i:3584 + 512 * i] for i in range(2)]
                 + [whole(A["attn_up"][0])] + [cut(w_out, 0), cut(w_out, 1)])
        Q_P, K_P, V_P, U_P, GA_P, PUP_P, GB_P, AUP_P, WO_P = 0, 1, 2, 3, 4, 6, 7, 9, 10
        FRONT = len(front)

        def slot(n, wide=False):
            if wide:
                return ring[:, n % SLOTS, :].rearrange("p (c n) -> p c n", c=4)
            return ring[:, n % SLOTS, :].rearrange("p (c n) -> p c n", c=NC)

        units = [(t, h) for t in range(NT) for h in range(HEADS)]
        STEPS_ATT = len(units) + 2
        strips = ([("qkv", i) for i in range(6)] + [("u", g) for g in range(NG)]
                  + [("gate", c) for c in range(NC)] + [("group", i) for i in range(2)]
                  + [("pup", c) for c in range(NC)] + [("gate", NC + c) for c in range(NC)]
                  + [("aup", c) for c in range(NC)])
        strip_no = {s: n for n, s in enumerate(strips)}

        def strip_bank(s):
            return ps[:, strip_no[s] % 2, :]

        def strip_wait(eng, s):
            eng.wait_ge(strip_done, strip_no[s] + 1)

        def strip_release(ins, s):
            ins.then_inc(strip_free[strip_no[s] % 2], 1)


        def strip_read(eng, s):
            eng.wait_ge(strip_free[strip_no[s] % 2], strip_no[s] // 2 + 1)

        def front_piece_free(eng, n):
            last = {Q_P: ("qkv", 1), K_P: ("qkv", 3), V_P: ("qkv", 5), U_P: ("u", 3), GA_P: ("gate", 3),
                    GA_P + 1: ("gate", 7), PUP_P: ("pup", NC - 1), GB_P: ("gate", 11), GB_P + 1: ("gate", 15),
                    AUP_P: ("aup", NC - 1)}
            if n in last:
                strip_wait(eng, last[n])
            else:
                eng.wait_ge(wo_done, 2 + n - WO_P + 1)

        @block.sync
        def _(sp):
            for t in range(NT):
                sp.dma_start(xt[:, t, :], A["x"][0, P * t:P * (t + 1), :]).then_inc(x_in[t], 16)
            for r0, src in rows:
                sp.dma_start(prow[r0:r0 + src.shape[0], :], src).then_inc(rows_in, 16)
            for n, src in enumerate(front):
                if n == 1:
                    for dst, par in params:
                        sp.dma_start(dst, par).then_inc(par_in, 16)
                if n >= SLOTS:
                    front_piece_free(sp, n - SLOTS)
                sp.dma_start(slot(n, wide=src.shape[1] == 4), src).then_inc(slot_in[n % SLOTS], 16)
                if n == SLOTS:
                    sp.wait_ge(qk_T, 4)
                    for t in range(NT):
                        sp.dma_start(xt[:, t, :], A["x"][0, P * t:P * (t + 1), :]).then_inc(x_again, 16)

            def expert_pieces(step, at, first=False):
                for j in range(UNROLL):
                    for m, name in enumerate(("exp_w_gate", "exp_w_up", "exp_w_down")):
                        w = A[name][0].rearrange("e (c p) n -> p e c n", p=P)
                        for half in range(2):
                            n = PIECES_PER_EXPERT * j + 2 * m + half
                            if first and n < SLOTS:
                                front_piece_free(sp, FRONT - SLOTS + n)
                            else:
                                sp.wait_ge(piece_done, at * (UNROLL * PIECES_PER_EXPERT) + (n - SLOTS + 1))
                            src = w[:, bass.ds(step * UNROLL + j, 1), 4 * half:4 * half + 4, :]
                            src = src.rearrange("p e c n -> p (e c) n")
                            sp.dma_start(slot(FRONT + n, wide=True), src).then_inc(slot_in[(FRONT + n) % SLOTS], 16)

            expert_pieces(0, 0, first=True)
            with sp.Fori(1, STEPS) as step:
                expert_pieces(step, step)
            sp.wait_ge(rounds_ready, 1)
            rounds = sp.value_load(rounds_i[0:1, 0:1], min_val=1, max_val=ROUNDS)
            with sp.If(rounds > 1):
                with sp.Fori(1, rounds) as r:
                    with sp.Fori(0, STEPS) as step:
                        expert_pieces(step, r * STEPS + step)
            for t in range(NT):
                for half in range(2):
                    part_cols = slice(HALF * half, HALF * (half + 1))
                    sp.wait_ge(out_ready, 2 * t + half + 1)
                    sp.dma_start(out[0, P * t:P * (t + 1), part_cols], xt[:, t, part_cols]).then_inc(out_done, 16)
            sp.wait_ge(out_done, 16 * 2 * NT)

        @block.tensor
        def _(pe):
            mm, tr = nc.tensor.matmul, nc.tensor.transpose

            def piece_wait(n):
                pe.wait_ge(slot_in[n % SLOTS], 16 * (n // SLOTS + 1))

            def strip_start(s):
                n = strip_no[s]
                if n >= 2:
                    pe.wait_ge(strip_free[n % 2], n // 2)

            pe.wait_ge(con_in, 16)
            pe.wait_ge(rows_in, 16 * 5)
            tr(ps[:, 0, 0:R_ROWS], prow[0:R_ROWS, :], ident[0:R_ROWS, 0:R_ROWS]).then_inc(cols_T, 1)
            for t in range(NT):
                pe.wait_ge(h_ready, t + 1)
                for q in range(2):
                    for c in range(4):
                        last = tr(ps[:, 2 + 2 * t + q, P * c:P * (c + 1)],
                                  xt[:, t, P * (4 * q + c):P * (4 * q + c + 1)], ident)
                    last.then_inc(h_T, 1)

            pe.wait_ge(hT_ready, 4)
            pe.wait_ge(cols_ready, 1)
            for i, piece in enumerate((Q_P, K_P, V_P)):
                piece_wait(piece)
                for t in range(NT):
                    s = ("qkv", 2 * i + t)
                    strip_start(s)
                    for c in range(NC):
                        last = mm(strip_bank(s), hT[:, c, P * t:P * (t + 1)], slot(piece)[:, c, :],
                                  start=(c == 0), stop=(c == NC - 1))
                    last.then_inc(strip_done, 1)

            for w in range(2):
                pe.wait_ge(qk_ready, NT * (w + 1))
                for t in range(NT):
                    for h in range(HEADS):
                        last = tr(ps[:, 4 + 2 * w + t, P * h:P * (h + 1)], qk_tok[:, w, t, P * h:P * (h + 1)], ident)
                    last.then_inc(qk_T, 1)

            def by_channel(s, piece, cc):
                strip_start(s)
                for c in range(NC):
                    last = mm(strip_bank(s)[:, 0:S], slot(piece)[:, c, P * cc:P * (cc + 1)], hT[:, c, :],
                              start=(c == 0), stop=(c == NC - 1))
                last.then_inc(strip_done, 1)

            def u_strip(g):
                if g == 0:
                    piece_wait(U_P)
                by_channel(("u", g), U_P, g)

            def gate_strip(c):
                piece = (GA_P if c < NC else GB_P) + (c % NC) // 4
                if c % 4 == 0:
                    piece_wait(piece)
                by_channel(("gate", c), piece, c % 4)

            u_strip(0)
            u_strip(1)
            fill = [lambda: u_strip(2), lambda: u_strip(3)] + [lambda c=c: gate_strip(c) for c in range(NC)]

            for step in range(STEPS_ATT):
                if step < len(units):
                    t, h = units[step]
                    keys = P * (t + 1)
                    if step == 0:
                        pe.wait_ge(q_moved, 2)
                        pe.wait_ge(k_moved, 2)
                        pe.wait_ge(mask_ready, 3)
                    if step >= 2:
                        pe.wait_ge(exp_ready, 2 * (step - 1))
                    for m in range(2):
                        b = 4 + 2 * (step % 2) + m
                        rows = slice(HD * m, HD * (m + 1))
                        mm(ps[:, b, 0:keys], qT[rows, h, P * t:P * (t + 1)], kT[rows, h, 0:keys],
                           start=True, stop=True)
                    for m in range(2):
                        b = 4 + 2 * (step % 2) + m
                        last = mm(ps[:, b, keys - CHUNK:keys], mask_q[:], mask_k[:],
                                  start=False, stop=True, skip_group_check=True)
                    last.then_inc(scored, 1)
                fill[step]()
                if 1 <= step <= len(units):
                    t, h = units[step - 1]
                    pe.wait_ge(diff_ready, step)
                    if step >= 2:
                        pe.wait_ge(diffT_ready, step - 1)
                    for kc in range(t + 1):
                        last = tr(ps[:, 2, P * kc:P * (kc + 1)], diff[:, (step - 1) % 2, P * kc:P * (kc + 1)], ident)
                    last.then_inc(diff_T, 1)
                if step >= 2:
                    t, h = units[step - 2]
                    pe.wait_ge(diffT_ready, step - 1)
                    if step == 2:
                        strip_read(pe, ("qkv", 4))
                        strip_read(pe, ("qkv", 5))
                    if step >= 3:
                        pe.wait_ge(o_ready, step - 2)
                    for kc in range(t + 1):
                        last = mm(ps[:, 3, 0:VD], diffT[:, step % 2, P * kc:P * (kc + 1)],
                                  vtok[:, kc, VD * h:VD * (h + 1)], start=(kc == 0), stop=(kc == t))
                    last.then_inc(o_done, 1)

            pe.wait_ge(par_in, 16 * PARAMS)
            pe.wait_ge(pooled, NG)
            for i in range(2):
                s = ("group", i)
                strip_start(s)
                for g in range(2):
                    last = mm(strip_bank(s)[:, S * g:S * (g + 1)], poolw[:, 2 * i + g, :], pT[:, 2 * i + g, :],
                              start=True, stop=True)
                last.then_inc(strip_done, 1)

            def up(kind, piece, src):
                piece_wait(piece)
                for m in range(NC):
                    strip_start((kind, m))
                    for k in range(4):
                        last = mm(strip_bank((kind, m))[:, 0:S], slot(piece, wide=True)[:, k, P * m:P * (m + 1)],
                                  src[:, k, :], start=(k == 0), stop=(k == 3))
                    last.then_inc(strip_done, 1)

            strip_read(pe, ("group", 0))
            strip_read(pe, ("group", 1))
            up("pup", PUP_P, yT)
            for c in range(NC, 2 * NC):
                gate_strip(c)

            for t in range(NT):
                pe.wait_ge(o_normed, t + 1)
                for h in range(HEADS):
                    last = tr(ps[:, 2 + t, P * h:P * (h + 1)], otok[:, t, VD * h:VD * (h + 1)], ident)
                last.then_inc(o_T, 1)
            pe.wait_ge(oT_ready, 2)
            up("aup", AUP_P, oT)

            piece_wait(WO_P)
            piece_wait(WO_P + 1)
            def project(t, half):
                for m in range(NC):
                    if t == 0 and half == 0:
                        pe.wait_ge(merged, m + 1)
                    last = mm(ps[:, 4 + 2 * t + half, :], gate[:, m, P * t:P * (t + 1)],
                              slot(WO_P + half)[:, m, :], start=(m == 0), stop=(m == NC - 1))
                last.then_inc(wo_done, 1)

            def turn_norm(t):
                for q in range(2):
                    pe.wait_ge(h2_ready, 2 * t + q + 1)
                    for c in range(4):
                        last = tr(ps[:, 2 * t + q, P * c:P * (c + 1)],
                                  h2[:, t, P * (4 * q + c):P * (4 * q + c + 1)], ident)
                    last.then_inc(h2_T, 1)

            project(0, 0)
            project(0, 1)
            project(1, 0)
            turn_norm(0)
            project(1, 1)
            turn_norm(1)
            pe.wait_ge(rw_ready, 1)
            pe.wait_ge(h2T_even, NT)
            pe.wait_ge(h2T_odd, NT)
            for k in range(2):
                for c in range(4):
                    last = mm(ps[E * c:E * (c + 1), 4, 0:S], rw[:, 4 * k + c, :], h2T[:, 4 * k + c, :],
                              start=(k == 0), stop=(k == 1))
            last.then_inc(logit_done, 1)
            pe.wait_ge(logitT_ready, 1)
            for t in range(NT):
                last = tr(ps[:, 6 + t, 0:P], logitT[:, P * t:P * (t + 1)], ident)
            last.then_inc(logit_T, 1)
            pe.wait_ge(chosen_ready, 1)
            mm(ps[:, 5, 0:E], tri, chosen[:, 0, :], start=True, stop=True)
            mm(ps[:, 5, E:2 * E], ones, chosen[:, 0, :], start=True, stop=False)
            mm(ps[:, 5, E:2 * E], tri, chosen[:, 1, :], start=False, stop=True).then_inc(rank_done, 1)
            for t in range(NT):
                last = mm(ps[0:1, 7, 0:E], ones[:, 0:1], chosen[:, t, :], start=(t == 0), stop=(t == NT - 1))
            last.then_inc(rank_done, 1)
            pe.wait_ge(zero_row, 1)
            for b in range(4):
                mm(ps[:, b, :], zrow[:, 0:P], zrow[:], start=True, stop=True)

            def gather(buf):
                for t in range(NT):
                    for half in range(2):
                        last = mm(ps[BLOCK * half:BLOCK * (half + 1), 6, :], pick[:, buf, t, :],
                                  h2[:, t, HALF * half:HALF * (half + 1)], start=(t == 0), stop=(t == NT - 1))
                last.then_inc(gathered, 1)

            def turn(bank, src):
                for c in range(4):
                    last = tr(ps[:, bank, P * c:P * (c + 1)], src[:, P * c:P * (c + 1)], ident)
                return last

            def scatter(signal=None):
                for t in range(NT):
                    for half in range(2):
                        rows = slice(BLOCK * half, BLOCK * (half + 1))
                        last = mm(ps[:, 2 * t + half, :], pickT[rows, P * t:P * (t + 1)], y_e[rows, :],
                                  start=False, stop=True, skip_group_check=True)
                        if signal:
                            last.then_inc(signal, 1)

            pe.wait_ge(pick_ready, 1)
            gather(0)
            pe.wait_ge(hg_ready, 1)
            turn(6, h_got).then_inc(h_turned, 1)
            pe.wait_ge(rows_zero, 1)
            pe.wait_ge(bias_in, 16 * 3)

            pe.wait_ge(rounds_ready, 1)
            rounds = pe.value_load(rounds_i[0:1, 0:1], min_val=1, max_val=ROUNDS)
            with pe.Fori(0, rounds) as r:
                with pe.Fori(0, STEPS) as step:
                    done = (r * STEPS + step) * UNROLL
                    landed = (r * STEPS + step) * (16 * UNROLL * PIECES_PER_EXPERT // SLOTS)
                    for j in range(UNROLL):
                        buf = j % 2

                        def product(k, bank, src):
                            n = FRONT + PIECES_PER_EXPERT * j + k
                            pe.wait_ge(slot_in[n % SLOTS], landed + 16 * (n // SLOTS + 1))
                            for c in range(4):
                                for half in range(2):
                                    last = mm(ps[BLOCK * half:BLOCK * (half + 1), bank, :], src[:, c, k % 2, :],
                                              slot(n, wide=True)[:, c, HALF * half:HALF * (half + 1)],
                                              start=False, stop=(k % 2 == 1 and c == 3))
                            last.then_inc(piece_done, 1)

                        def biases(k, bank):
                            for half in range(2):
                                mm(ps[BLOCK * half:BLOCK * (half + 1), bank, :], this_e[:, buf, k, :],
                                   bias_rows[:, HALF * half:HALF * (half + 1)], start=True, stop=False)

                        biases(0, 4)
                        pe.wait_ge(h_in_ready, done + (j + 1))
                        product(0, 4, h_in[:, buf])
                        product(1, 4, h_in[:, buf])
                        pe.wait_ge(y_ready, done + (j + 1))
                        pe.wait_ge(pickT_ready, done + (j + 1))
                        scatter()
                        biases(1, 5)
                        product(2, 5, h_in[:, buf])
                        pe.wait_ge(pick_ready, done + (j + 2))
                        gather(1 - buf)
                        product(3, 5, h_in[:, buf])
                        pe.wait_ge(hg_ready, done + (j + 2))
                        turn(6, h_got).then_inc(h_turned, 1)
                        pe.wait_ge(act_ready, done + (j + 1))
                        turn(7, act_out).then_inc(act_T, 1)
                        for t in range(NT):
                            last = tr(ps[:, 5, P * t:P * (t + 1)], pickw[:, buf, t].rearrange("p h s -> p (h s)"), ident)
                        last.then_inc(pick_T, 1)
                        pe.wait_ge(actT_ready, done + (j + 1))
                        biases(2, 7)
                        product(4, 7, actT)
                        product(5, 7, actT)
            pe.wait_ge(pickT_ready, rounds * E + 1)
            pe.wait_ge(y_ready, rounds * E + 1)
            scatter(signal=scattered)

        @block.scalar
        def _(act):
            fn = nc.scalar.activation
            act.dma_start(con[:], consts).then_inc(con_in, 16)
            act.wait_ge(zero_col, 1)
            fn(scrap[:, 1:2], scrap[:, 0:1], ACT.Sqrt)

            for t in range(NT):
                act.wait_ge(x_in[t], 16)
                fn(junk[:, t, :], xt[:, t, :], ACT.Square, accum_out=ss[:, t:t + 1]).then_inc(x_sq, 1)
            for t in range(NT):
                act.wait_ge(x_var, t + 1)
                fn(rstd[:, t:t + 1], rstd[:, t:t + 1], ACT.Sqrt).then_inc(x_std, 1)

            for i in range(4):
                w, t = divmod(i, NT)
                s = ("qkv", i)
                strip_wait(act, s)
                if t == 0 and w == 0:
                    act.wait_ge(h_T, 4)
                nc.scalar.copy(qk_tok[:, w, t, :], strip_bank(s))
                if i >= 2:
                    act.wait_ge(qk_var, i - 1)
                strip_release(fn(squares[:, i % 2, :], strip_bank(s), ACT.Square), s)
                act.wait_ge(qk_var, i + 1)
                fn(qrs[:, i, :], qrs[:, i, :], ACT.Sqrt).then_inc(qk_std, 1)
            for t in range(NT):
                s = ("qkv", 4 + t)
                strip_wait(act, s)
                strip_release(nc.scalar.copy(vtok[:, t, :], strip_bank(s)), s)
            act.wait_ge(lam_sum, 1)
            fn(lam2, lam2, ACT.Exp).then_inc(lam_exp, 1)
            for t in range(NT):
                act.wait_ge(qk_T, t + 1)
                nc.scalar.copy(qT[:, :, P * t:P * (t + 1)],
                               ps[:, 4 + t, :].rearrange("p (h s) -> p h s", h=HEADS)).then_inc(q_moved, 1)

            def u_copy(g):
                s = ("u", g)
                strip_wait(act, s)
                strip_release(nc.scalar.copy(uT[:, g, PAD:], strip_bank(s)[:, 0:S]), s)

            def gate_e(c):
                s = ("gate", c)
                strip_wait(act, s)
                strip_release(fn(gate[:, c, :], strip_bank(s)[:, 0:S], ACT.Exp, bias=ngate[:, c:c + 1], scale=-1.0), s)

            u_copy(0)
            u_copy(1)
            fill = [lambda: u_copy(2), lambda: u_copy(3)] + [lambda c=c: gate_e(c) for c in range(NC)]
            for step in range(STEPS_ATT):
                b = step % 2
                if step < len(units):
                    t, h = units[step]
                    keys = P * (t + 1)
                    act.wait_ge(max_ready, step + 1)
                    for m in range(2):
                        fn(prob[:, b, m, 0:keys], ps[:, 4 + 2 * b + m, 0:keys], ACT.Exp, bias=mx[:, b, m:m + 1],
                           scale=HD ** -0.5, accum_out=den[:, b, m:m + 1]).then_inc(exp_ready, 1)
                fill[step]()
                if 1 <= step <= len(units):
                    t, h = units[step - 1]
                    act.wait_ge(diff_T, step)
                    nc.scalar.copy(diffT[:, (step - 1) % 2, 0:P * (t + 1)], ps[:, 2, 0:P * (t + 1)]).then_inc(diffT_ready, 1)
                if step >= 2:
                    t, h = units[step - 2]
                    act.wait_ge(o_done, step - 1)
                    nc.scalar.copy(otok[:, t, VD * h:VD * (h + 1)], ps[:, 3, 0:VD])
                    fn(junk_o[:], ps[:, 3, 0:VD], ACT.Square, accum_out=oss[:, step - 2:step - 1]).then_inc(o_ready, 1)
            for i in range(2):
                s = ("group", i)
                strip_wait(act, s)
                for g in range(2):
                    last = fn(yT[:, 2 * i + g, :], strip_bank(s)[:, S * g:S * (g + 1)], ACT.Copy,
                              scale=cols[:, R_PSCALE + 2 * i + g:R_PSCALE + 2 * i + g + 1])
                strip_release(last, s)
            act.wait_ge(o_var, 1)
            fn(ors, ors, ACT.Sqrt).then_inc(o_std, 1)
            for c in range(NC, 2 * NC):
                gate_e(c)
            for t in range(NT):
                act.wait_ge(o_T, t + 1)
                fn(oT[:, :, P * t:P * (t + 1)], ps[:, 2 + t, :].rearrange("p (h s) -> p h s", h=HEADS), ACT.Copy,
                   scale=subln8).then_inc(oT_ready, 1)

            def squares2(t, half):
                act.wait_ge(x2_ready, 2 * t + half + 1)
                fn(junk[:, t, HALF * half:HALF * (half + 1)], xt[:, t, HALF * half:HALF * (half + 1)], ACT.Square,
                   accum_out=ss2[:, t, half:half + 1]).then_inc(x2_sq, 1)

            def root2(t):
                act.wait_ge(x2_var, t + 1)
                fn(rstd[:, t:t + 1], rstd[:, t:t + 1], ACT.Sqrt).then_inc(x2_std, 1)

            def turned(t):
                act.wait_ge(h2_T, 2 * t + 2)
                nc.scalar.copy(h2T[:, 4:8, P * t:P * (t + 1)],
                               ps[:, 2 * t + 1, :].rearrange("p (c s) -> p c s", c=4)).then_inc(h2T_odd, 1)

            squares2(0, 0)
            for k, name in enumerate(("exp_b_gate", "exp_b_up", "exp_b_down")):
                act.dma_start(bias_rows[E * k:E * (k + 1), :], A[name][0]).then_inc(bias_in, 16)
            squares2(0, 1)
            root2(0)
            squares2(1, 0)
            turned(0)
            squares2(1, 1)
            root2(1)
            turned(1)
            act.wait_ge(logit_done, 1)
            nc.scalar.copy(logitT, ps[:, 4, 0:S]).then_inc(logitT_ready, 1)
            act.wait_ge(top_ready, 1)
            fn(topw[:], topw[:], ACT.Exp).then_inc(top_exp, 1)
            act.wait_ge(gathered, 1)
            nc.scalar.copy(h_got, ps[:, 6, :]).then_inc(hg_ready, 1)
            act.wait_ge(rounds_ready, 1)
            rounds = act.value_load(rounds_i[0:1, 0:1], min_val=1, max_val=ROUNDS)
            with act.Fori(0, rounds) as r:
                with act.Fori(0, STEPS) as step:
                    done = (r * STEPS + step) * UNROLL
                    for j in range(UNROLL):
                        act.wait_ge(g_ready, done + (j + 1))
                        fn(sig, g1, ACT.Sigmoid, scale=ALPHA).then_inc(sig_ready, 1)
                        act.wait_ge(gathered, done + (j + 2))
                        nc.scalar.copy(h_got, ps[:, 6, :]).then_inc(hg_ready, 1)
                        act.wait_ge(act_T, done + (j + 1))
                        nc.scalar.copy(actT.rearrange("p c h s -> p (c h s)"), ps[:, 7, :]).then_inc(actT_ready, 1)
                        act.wait_ge(pick_T, done + (j + 1))
                        nc.scalar.copy(pickT, ps[:, 5, 0:S]).then_inc(pickT_ready, 1)
                        act.wait_ge(piece_done, done * PIECES_PER_EXPERT + (PIECES_PER_EXPERT * j + 6))
                        nc.scalar.copy(y_e, ps[:, 7, :]).then_inc(y_ready, 1)

        @block.gpsimd
        def _(pool):
            steps = [0]

            def own(ins):
                steps[0] += 1
                ins.then_inc(pool_step, 1)
                pool.wait_ge(pool_step, steps[0])

            gp = nc.gpsimd
            own(gp.memset(uT[:, :, 0:PAD], 0.0))
            gp.memset(mask_q[:, 0:CHUNK], 1.0).then_inc(mask_ready, 1)
            gp.memset(mask_q[:, CHUNK:], 0.0).then_inc(mask_ready, 1)
            gp.memset(mask_k[:], MASKED).then_inc(mask_ready, 1)
            pool.wait_ge(mask_ready, 3)
            gp.memset(zrow[:], 0.0).then_inc(zero_row, 1)
            pool.wait_ge(zero_row, 1)
            pool.wait_ge(con_in, 16)
            for g in range(NG):
                strip_read(pool, ("u", g))
                cur = uT[:, g, :]
                for k in range(g + 1):
                    lo, shift = (2 << k) - 1, 1 << k
                    nxt = sums[:, k % 2, :]
                    own(gp.tensor_tensor(nxt[:, lo:], cur[:, lo:], cur[:, lo - shift:S + PAD - shift], ALU.add))
                    cur = nxt
                gp.tensor_scalar(pT[:, g, 16:], cur[:, PAD + 16:], 1.0 / (2 << g), None, ALU.mult)
                own(gp.tensor_tensor(pT[:, g, 0:16], cur[:, PAD:PAD + 16], con[:, C_INV + 16 * g:C_INV + 16 * g + 16],
                                     ALU.mult))
                gp.tensor_tensor(pT[:, g, :], pT[:, g, :], uT[:, g, PAD:], ALU.subtract).then_inc(pooled, 1)
            pool.wait_ge(wo_done, 1)
            gp.memset(y_e, 0.0).then_inc(y_ready, 1)
            pool.wait_ge(y_ready, 1)
            gp.memset(pickT, 0.0).then_inc(pickT_ready, 1)
            pool.wait_ge(pickT_ready, 1)
            gp.memset(bias_rows[3 * E:, :], 0.0).then_inc(rows_zero, 1)

        @block.vector
        def _(dve):
            v = nc.vector
            steps = [0]

            def own(ins):
                steps[0] += 1
                ins.then_inc(dve_step, 1)
                dve.wait_ge(dve_step, steps[0])

            def wide(col, shape, axis):
                return col.unsqueeze(axis).broadcast_to(shape)

            v.memset(scrap[:, 0:1], 1.0).then_inc(zero_col, 1)
            for t in range(NT):
                dve.wait_ge(x_sq, t + 1)
                v.tensor_scalar(rstd[:, t:t + 1], ss[:, t:t + 1], 1.0 / D, EPS, ALU.mult, ALU.add).then_inc(x_var, 1)
            for t in range(NT):
                dve.wait_ge(x_std, t + 1)
                own(v.reciprocal(rstd[:, t:t + 1], rstd[:, t:t + 1]))
                v.tensor_scalar(xt[:, t, :], xt[:, t, :], rstd[:, t:t + 1], None, ALU.mult).then_inc(h_ready, 1)
            dve.wait_ge(cols_T, 1)
            v.tensor_copy(cols[:], ps[:, 0, 0:R_ROWS]).then_inc(cols_ready, 1)
            dve.wait_ge(cols_ready, 1)
            v.tensor_scalar(ngate, cols[:, R_BGATE:R_BGATE + 2 * NC], -1.0, None, ALU.mult)
            own(v.tensor_scalar(subln8, cols[:, R_SUBLN:R_SUBLN + 1], 1.0 - LAM_INIT, None, ALU.mult))
            for t in range(NT):
                for q in range(2):
                    dve.wait_ge(h_T, 2 * t + q + 1)
                    v.tensor_tensor(hT[:, 4 * q:4 * q + 4, P * t:P * (t + 1)],
                                    ps[:, 2 + 2 * t + q, :].rearrange("p (c s) -> p c s", c=4),
                                    wide(cols[:, R_MIXG + 4 * q:R_MIXG + 4 * q + 4], [P, 4, P], 2),
                                    ALU.mult).then_inc(hT_ready, 1)
            dve.wait_ge(par_in, 16 * PARAMS)
            own(v.tensor_tensor(lamv[:, 0:2, :], lamv[:, 0:2, :], lamv[:, 2:4, :], ALU.mult))
            v.tensor_reduce(lam2, lamv[:, 0:2, :], AX.X, ALU.add).then_inc(lam_sum, 1)

            for i in range(4):
                w, t = divmod(i, NT)
                strip_read(dve, ("qkv", i))
                own(v.tensor_reduce(qss[:, i, :], squares[:, i % 2, :].rearrange("p (g d) -> p g d", d=HD), AX.X, ALU.add))
                v.tensor_scalar(qrs[:, i, :], qss[:, i, :], 1.0 / HD, EPS, ALU.mult, ALU.add).then_inc(qk_var, 1)
                dve.wait_ge(qk_std, i + 1)
                own(v.reciprocal(qrs[:, i, :], qrs[:, i, :]))
                z = qk_tok[:, w, t, :].rearrange("p (g d) -> p g d", d=HD)
                own(v.tensor_tensor(z, z, wide(qrs[:, i, :], [P, 8, HD], 2), ALU.mult))
                own(v.tensor_tensor(z, z, wide((gq, gk)[w], [P, 8, HD], 1), ALU.mult))
                cosb = wide(con[:, C_COS + 8 * t:C_COS + 8 * t + 8], [P, 8, 8], 1)
                sinb = wide(con[:, C_SIN + 8 * t:C_SIN + 8 * t + 8], [P, 8, 8], 1)
                v.tensor_tensor(ropeb[:, :, 0:8], z[:, :, 8:16], sinb, ALU.mult)
                own(v.tensor_tensor(ropeb[:, :, 8:16], z[:, :, 0:8], sinb, ALU.mult))
                v.tensor_tensor(z[:, :, 0:8], z[:, :, 0:8], cosb, ALU.mult)
                own(v.tensor_tensor(z[:, :, 8:16], z[:, :, 8:16], cosb, ALU.mult))
                own(v.tensor_tensor(z[:, :, 0:8], z[:, :, 0:8], ropeb[:, :, 0:8], ALU.subtract))
                v.tensor_tensor(z[:, :, 8:16], z[:, :, 8:16], ropeb[:, :, 8:16], ALU.add).then_inc(qk_ready, 1)
            for t in range(NT):
                dve.wait_ge(qk_T, NT + t + 1)
                v.tensor_copy(kT[:, :, P * t:P * (t + 1)],
                              ps[:, 6 + t, :].rearrange("p (h s) -> p h s", h=HEADS)).then_inc(k_moved, 1)
            dve.wait_ge(lam_exp, 1)
            own(v.tensor_tensor(neglam, lam2[:, 1:2], lam2[:, 0:1], ALU.subtract))
            own(v.tensor_scalar(neglam, neglam, -LAM_INIT, None, ALU.add))

            def sigmoid_rest(c):
                strip_read(dve, ("gate", c))
                own(v.tensor_scalar(gate[:, c, :], gate[:, c, :], 1.0, None, ALU.add))
                return v.reciprocal(gate[:, c, :], gate[:, c, :])

            for step in range(len(units)):
                t, h = units[step]
                b, keys = step % 2, P * (t + 1)
                dve.wait_ge(scored, step + 1)
                own(v.tensor_reduce(mx[:, b, :], ps[:, 4 + 2 * b:6 + 2 * b, 0:keys], AX.X, ALU.max))
                v.tensor_scalar(mx[:, b, :], mx[:, b, :], -HD ** -0.5, None, ALU.mult).then_inc(max_ready, 1)
                dve.wait_ge(exp_ready, 2 * step + 2)
                own(v.reciprocal(den[:, b, :], den[:, b, :]))
                own(v.tensor_tensor(den[:, b, 1:2], den[:, b, 1:2], neglam, ALU.mult))
                own(v.tensor_scalar(prob[:, b, 1, 0:keys], prob[:, b, 1, 0:keys], den[:, b, 1:2], None, ALU.mult))
                v.scalar_tensor_tensor(out=diff[:, b, 0:keys], in0=prob[:, b, 0, 0:keys], scalar=den[:, b, 0:1],
                                       in1=prob[:, b, 1, 0:keys], op0=ALU.mult, op1=ALU.add).then_inc(diff_ready, 1)
                if step >= 2:
                    own(sigmoid_rest(step - 2))
            for c in range(len(units) - 2, NC):
                own(sigmoid_rest(c))

            dve.wait_ge(o_ready, len(units))
            v.tensor_scalar(ors, oss, 1.0 / VD, EPS, ALU.mult, ALU.add).then_inc(o_var, 1)
            dve.wait_ge(o_std, 1)
            own(v.reciprocal(ors, ors))
            for t in range(NT):
                z = otok[:, t, :].rearrange("p (h d) -> p h d", h=HEADS)
                v.tensor_tensor(z, z, wide(ors[:, HEADS * t:HEADS * (t + 1)], [P, HEADS, VD], 2),
                                ALU.mult).then_inc(o_normed, 1)
            for m in range(NC):
                s = ("pup", m)
                strip_wait(dve, s)
                strip_release(v.tensor_tensor(gate[:, m, :], strip_bank(s)[:, 0:S], gate[:, m, :], ALU.mult), s)
            for c in range(NC, 2 * NC):
                own(sigmoid_rest(c))
            for m in range(NC):
                s = ("aup", m)
                strip_wait(dve, s)
                strip_release(v.tensor_tensor(gate[:, NC + m, :], strip_bank(s)[:, 0:S], gate[:, NC + m, :], ALU.mult), s)
                strip_read(dve, s)
                v.tensor_tensor(gate[:, m, :], gate[:, m, :], gate[:, NC + m, :], ALU.add).then_inc(merged, 1)

            dve.wait_ge(x_again, 16 * NT)

            def residual(t, half):
                dve.wait_ge(wo_done, 2 * t + half + 1)
                z = xt[:, t, HALF * half:HALF * (half + 1)]
                v.tensor_tensor(z, z, ps[:, 4 + 2 * t + half, :], ALU.add).then_inc(x2_ready, 1)

            def normed(t):
                dve.wait_ge(x2_sq, 2 * t + 2)
                own(v.tensor_tensor(ss[:, t:t + 1], ss2[:, t, 0:1], ss2[:, t, 1:2], ALU.add))
                v.tensor_scalar(rstd[:, t:t + 1], ss[:, t:t + 1], 1.0 / D, EPS, ALU.mult, ALU.add).then_inc(x2_var, 1)
                dve.wait_ge(x2_std, t + 1)
                own(v.reciprocal(rstd[:, t:t + 1], rstd[:, t:t + 1]))
                for half in range(2):
                    part_cols = slice(HALF * half, HALF * (half + 1))
                    v.tensor_scalar(h2[:, t, part_cols], xt[:, t, part_cols], rstd[:, t:t + 1], None, ALU.mult).then_inc(h2_ready, 1)

            def turned(t):
                dve.wait_ge(h2_T, 2 * t + 1)
                v.tensor_copy(h2T[:, 0:4, P * t:P * (t + 1)],
                              ps[:, 2 * t, :].rearrange("p (c s) -> p c s", c=4)).then_inc(h2T_even, 1)

            residual(0, 0)
            residual(0, 1)
            normed(0)
            v.tensor_tensor(rw, rw, wide(cols[:, R_FFNG:R_FFNG + NC], [P, NC, E], 2), ALU.mult).then_inc(rw_ready, 1)
            residual(1, 0)
            turned(0)
            residual(1, 1)
            normed(1)
            turned(1)

            dve.wait_ge(logit_T, 1)
            own(v.tensor_reduce(logit, ps[:, 6:8, 0:P].rearrange("p t (g e) -> p t e g", g=4), AX.X, ALU.add))
            own(v.tensor_tensor(logit, logit, wide(rb, [P, NT, E], 1), ALU.add))
            for t in range(NT):
                last = v.max(top[:, t, :], logit[:, t, :])
            own(last)
            v.tensor_tensor(topw[:], top[:, :, 0:TOPK], top[:, :, 0:1].broadcast_to([P, NT, TOPK]),
                            ALU.subtract).then_inc(top_ready, 1)
            for t in range(NT):
                last = v.max_index(topi[:, t, :], top[:, t, :], logit[:, t, :])
            own(last)
            own(v.tensor_copy(topf[:], topi[:]))
            for t in range(NT):
                last = v.tensor_tensor(eq4[:, t], wide(iota[:, 0:E], [P, TOPK, E], 1),
                                       wide(topf[:, t, 0:TOPK], [P, TOPK, E], 2), ALU.is_equal)
            own(last)
            v.tensor_reduce(chosen, eq4.rearrange("p t k e -> p t e k"), AX.X, ALU.add).then_inc(chosen_ready, 1)
            dve.wait_ge(top_exp, 1)
            own(v.tensor_reduce(psum4, topw[:], AX.X, ALU.add))
            own(v.reciprocal(psum4, psum4))
            own(v.tensor_tensor(topw[:], topw[:], wide(psum4, [P, NT, TOPK], 2), ALU.mult))
            dve.wait_ge(rank_done, 1)
            own(v.tensor_tensor(ranks, ps[:, 5, 0:2 * E].rearrange("p (t e) -> p t e", t=NT), chosen, ALU.mult))
            for r in range(ROUNDS + 1):
                last = v.tensor_scalar(rank_tab[:, :, E * r:E * (r + 1)], ranks, -1.0 - BLOCK * r, None, ALU.add)
            own(last)

            def select(n, buf):
                for t in range(NT):
                    v.tensor_scalar(pick[:, buf, t, :], iota, rank_tab[:, t, bass.ds(n, 1)], None, ALU.is_equal)

            def weigh(n, buf):
                for t in range(NT):
                    v.tensor_scalar(pickw[:, buf, t], wide(iota, [P, 2, BLOCK], 1), rank_tab[:, t, bass.ds(n, 1)],
                                    comb_tab[:, t, bass.ds(n, 1)], ALU.is_equal, ALU.mult)

            def name_expert(e, buf):
                for k in range(3):
                    last = v.tensor_copy(this_e[:, buf, k, :],
                                         con[:, bass.ds(e + (C_IDENT + E * k), 1)].broadcast_to([P, BLOCK]))
                last.then_inc(pick_ready, 1)

            select(0, 0)
            name_expert(0, 0)
            dve.wait_ge(rank_done, 2)
            own(v.tensor_reduce(cnt, ps[0:1, 7, 0:E], AX.X, ALU.max))
            own(v.tensor_scalar(cnt2[:, 0:1], cnt, float(BLOCK), 1.0, ALU.is_gt, ALU.add))
            own(v.scalar_tensor_tensor(out=cnt2[:, 1:2], in0=cnt, scalar=2.0 * BLOCK, in1=cnt2[:, 0:1],
                                       op0=ALU.is_gt, op1=ALU.add))
            v.scalar_tensor_tensor(out=rounds_i[:], in0=cnt, scalar=3.0 * BLOCK, in1=cnt2[:, 1:2],
                                   op0=ALU.is_gt, op1=ALU.add).then_inc(rounds_ready, 1)

            for t in range(NT):
                last = v.tensor_tensor(eq4w[:, t], eq4[:, t], wide(topw[:, t, :], [P, TOPK, E], 2), ALU.mult)
            own(last)
            own(v.tensor_reduce(combf, eq4w.rearrange("p t k e -> p t e k"), AX.X, ALU.add))
            own(v.tensor_copy(comb_tab.rearrange("p t (r e) -> p t r e", e=E),
                          combf.unsqueeze(2).broadcast_to([P, NT, ROUNDS + 1, E])))
            weigh(0, 0)

            def gathered_in(buf):
                gain = cols[:, R_FFNG:R_FFNG + NC].rearrange("p (h c) -> p c h", h=2)
                v.tensor_tensor(h_in[:, buf], ps[:, 6, :].rearrange("p (c h s) -> p c h s", c=4, h=2),
                                wide(gain, [P, 4, 2, BLOCK], 3), ALU.mult).then_inc(h_in_ready, 1)

            dve.wait_ge(h_turned, 1)
            gathered_in(0)

            dve.wait_ge(rounds_ready, 1)
            rounds = dve.value_load(rounds_i[0:1, 0:1], min_val=1, max_val=ROUNDS)
            with dve.Fori(0, rounds) as r:
                with dve.Fori(0, STEPS) as step:
                    done = (r * STEPS + step) * UNROLL
                    after = ((step + 1) & (STEPS - 1)) * UNROLL
                    for j in range(UNROLL):
                        dve.wait_ge(piece_done, done * PIECES_PER_EXPERT + (PIECES_PER_EXPERT * j + 2))
                        v.tensor_scalar(g1, ps[:, 4, :], LIMIT, None, ALU.min).then_inc(g_ready, 1)
                        e = (step * UNROLL + (j + 1)) if j < UNROLL - 1 else after
                        select(done + (j + 1), 1 - j % 2)
                        weigh(done + (j + 1), 1 - j % 2)
                        name_expert(e, 1 - j % 2)
                        dve.wait_ge(sig_ready, done + (j + 1))
                        v.tensor_tensor(gs, g1, sig, ALU.mult).then_inc(expert_step, 1)
                        dve.wait_ge(piece_done, done * PIECES_PER_EXPERT + (PIECES_PER_EXPERT * j + 4))
                        v.tensor_scalar(u1, ps[:, 5, :], LIMIT, -LIMIT, ALU.min, ALU.max).then_inc(expert_step, 1)
                        dve.wait_ge(expert_step, done * 2 + (2 * j + 2))
                        v.scalar_tensor_tensor(out=act_out, in0=u1, scalar=1.0, in1=gs, op0=ALU.add,
                                               op1=ALU.mult).then_inc(act_ready, 1)
                        dve.wait_ge(h_turned, done + (j + 2))
                        gathered_in(1 - j % 2)
            for t in range(NT):
                for half in range(2):
                    dve.wait_ge(scattered, 2 * t + half + 1)
                    z = xt[:, t, HALF * half:HALF * (half + 1)]
                    v.tensor_tensor(z, z, ps[:, 2 * t + half, :], ALU.add).then_inc(out_ready, 1)


_INS = ["x", "mix_norm_g", "w_in", "b_branch_gate", "pool_w", "pool_scale", "pool_up", "q_norm_g", "k_norm_g",
        "lambda_q1", "lambda_k1", "lambda_q2", "lambda_k2", "subln_g", "attn_up", "w_out", "ffn_norm_g",
        "router_w", "router_b", "exp_w_gate", "exp_b_gate", "exp_w_up", "exp_b_up", "exp_w_down", "exp_b_down"]


def kernel(**inputs):
    import concourse.bacc as _bacc
    from concourse.bass_utils import run_bass_kernel_spmd as _run

    nc = _bacc.Bacc("TRN2", target_bir_lowering=False, num_devices=1)
    arrays, aps = {}, {}
    for name in _INS:
        a = np.ascontiguousarray(inputs[name])
        arrays["in_" + name] = a
        aps[name] = nc.dram_tensor("in_" + name, a.shape, mybir.dt.from_np(a.dtype), kind="ExternalInput").ap()
    arrays["shape_constants"] = shape_constants()
    consts = nc.dram_tensor("shape_constants", (P, C_WIDTH), F32, kind="ExternalInput").ap()
    out = nc.dram_tensor("out", (1, S, D), F32, kind="ExternalOutput").ap()
    build(nc, aps, consts, out)
    r = _run(nc, [arrays], core_ids=[0])
    return r.results[0]["out"]
```

```python
from contextlib import ExitStack

import numpy as np

import concourse.bass as bass
from concourse import mybir

ALU = mybir.AluOpType
ACT = mybir.ActivationFunctionType
AX = mybir.AxisListType
F32 = mybir.dt.float32
F32R = mybir.dt.float32r
BF16 = mybir.dt.bfloat16
I32 = mybir.dt.int32
U32 = mybir.dt.uint32

P = 128
D = 1024
S = 256
NT = S // P
NC = D // P
HEADS, HD, VD = 4, 64, 128
QK = HEADS * 2 * HD
POOLW = 512
NG = 4
PAD = 16
CHUNK = 64
ROT = HD // 4
E = 32
TOPK = 4
F = 1024
EPS = 1e-6
LIMIT, ALPHA = 7.0, 1.702
LAM_INIT = 0.8 - 0.6
MASKED = -1e30

HALF = 512
SLOTS = 8
PIECE = NC * HALF
BLOCK = 64
ROUNDS = S // BLOCK
UNROLL = 4
STEPS = E // UNROLL
PIECES_PER_EXPERT = 6
ARENA = 16400

C_IDENT, C_TRI, C_ONES, C_IOTA, C_INV, C_COS, C_SIN, C_WIDTH = 0, 128, 256, 384, 448, 512, 528, 544
R_MIXG, R_BGATE, R_PSCALE, R_SUBLN, R_FFNG, R_ROWS = 0, 8, 24, 28, 29, 37


def shape_constants():
    c = np.zeros((P, C_WIDTH), np.float32)
    c[:, C_IDENT:C_IDENT + P] = np.eye(P)
    c[:, C_TRI:C_TRI + P] = np.triu(np.ones((P, P)))
    c[:, C_ONES:C_ONES + P] = 1.0
    c[:, C_IOTA:C_IOTA + BLOCK] = np.arange(BLOCK)
    for g in range(NG):
        c[:, C_INV + 16 * g:C_INV + 16 * (g + 1)] = 1.0 / np.minimum(np.arange(1, 17), 2 << g)
    inv = (np.float32(500000.0) ** (-np.arange(0, ROT, 2, dtype=np.float32) / np.float32(ROT))).astype(np.float32)
    ang = np.arange(S, dtype=np.float32)[:, None] * inv[None, :]
    for t in range(NT):
        c[:, C_COS + 8 * t:C_COS + 8 * t + 8] = np.cos(ang[P * t:P * (t + 1)])
        c[:, C_SIN + 8 * t:C_SIN + 8 * t + 8] = np.sin(ang[P * t:P * (t + 1)])
    return c


def build(nc, A, consts, out):
    with ExitStack() as ctx:
        def sb(name, shape, dt=F32):
            return ctx.enter_context(nc.sbuf_tensor(name, shape, dt))

        def sem(name):
            return ctx.enter_context(nc.semaphore(name))

        ps = ctx.enter_context(nc.psum_tensor("ps", [P, 8, HALF], F32))

        with ExitStack() as same_place:
            ring_r = [same_place.enter_context(nc.sbuf_tensor(f"ring_r{k}", [P, PIECE], F32R)) for k in range(SLOTS)]
        ring = sb("ring", [P, SLOTS, PIECE])
        xt = sb("xt", [P, NT, D])
        qk_tok = xt[:].rearrange("p t (w c) -> p w t c", w=2)
        con = sb("con", [P, C_WIDTH])
        cols = sb("cols", [P, R_ROWS])
        small = sb("small", [P, 256])
        with nc.sbuf_tensor("arena_r", [P, ARENA], F32R) as arena_r:
            pass
        arena = sb("arena", [P, ARENA])
        ident = con[:, C_IDENT:C_IDENT + P]
        tri = con[:, C_TRI:C_TRI + P]
        ones = con[:, C_ONES:C_ONES + P]
        iota = con[:, C_IOTA:C_IOTA + BLOCK]

        taken = [0]

        def part(n):
            at = taken[0]
            taken[0] += n
            assert taken[0] <= ARENA, taken[0]
            return arena[:, at:at + n]

        places = {}

        hT = part(NC * S).rearrange("p (c s) -> p c s", c=NC)
        places["q"] = taken[0]
        qT = part(HEADS * S).rearrange("p (h s) -> p h s", h=HEADS)
        places["k"] = taken[0]
        kT = part(HEADS * S).rearrange("p (h s) -> p h s", h=HEADS)
        places["gate"] = taken[0]
        gate = part(2 * NC * S).rearrange("p (c s) -> p c s", c=2 * NC)
        vtok = part(NT * 512).rearrange("p (t c) -> p t c", t=NT)
        places["u"] = taken[0]
        uT = part(NG * (S + PAD)).rearrange("p (g s) -> p g s", g=NG)
        places["p"] = taken[0]
        pT = part(NG * S).rearrange("p (g s) -> p g s", g=NG)
        sums = part(2 * (S + PAD)).rearrange("p (b s) -> p b s", b=2)
        prob = part(2 * 2 * S).rearrange("p (b m s) -> p b m s", b=2, m=2)
        diff = part(2 * S).rearrange("p (b s) -> p b s", b=2)
        diffT = part(2 * S).rearrange("p (b s) -> p b s", b=2)
        otok_flat = part(NT * 512)
        otok = otok_flat.rearrange("p (t c) -> p t c", t=NT)

        def pair(hi, lo, chunks):
            return tuple(arena_r[:, a:a + chunks * S].rearrange("p (c s) -> p c s", c=chunks) for a in (hi, lo))

        o_split = pair(places["q"], places["k"], HEADS)
        y_split = pair(places["u"], places["p"], NG)
        m_split = pair(places["gate"], places["gate"] + NC * S, NC)
        prow = otok_flat[:, 0:P]
        lamv = otok_flat[:, P:P + 4 * HD].rearrange("p (i d) -> p i d", i=4)
        squares = prob.rearrange("p b m s -> p b (m s)")
        junk = gate[:, NC:, :].rearrange("p (t c) s -> p t (c s)", t=NT)
        first_end = taken[0]
        gq = part(HD)
        gk = part(HD)
        poolw = part(NG * P).rearrange("p (g d) -> p g d", g=NG)
        rw = part(NC * E).rearrange("p (c e) -> p c e", c=NC)
        rb = part(E)
        h2 = hT.rearrange("p c s -> p (c s)").rearrange("p (t d) -> p t d", t=NT)
        taken[0] = NC * S
        x2T = part(NC * S).rearrange("p (c s) -> p c s", c=NC)
        h_in = part(2 * NC * BLOCK).rearrange("p (b c h s) -> p b c h s", b=2, c=4, h=2)
        h_got = part(HALF)
        g1 = part(HALF)
        sig = part(HALF)
        gs = part(HALF)
        u1 = part(HALF)
        act_out = part(HALF)
        actT = part(NC * BLOCK).rearrange("p (c h s) -> p c h s", c=4, h=2)
        y_e = part(HALF)
        pickT = part(S)
        pick = part(2 * NT * BLOCK).rearrange("p (b t s) -> p b t s", b=2, t=NT)
        pickw = part(2 * NT * 2 * BLOCK).rearrange("p (b t h s) -> p b t h s", b=2, t=NT, h=2)
        this_e = part(2 * 3 * BLOCK).rearrange("p (b k s) -> p b k s", b=2, k=3)
        bias_rows = part(D)
        rank_tab = part(NT * (ROUNDS + 1) * E).rearrange("p (t n) -> p t n", t=NT)
        comb_tab = part(NT * (ROUNDS + 1) * E).rearrange("p (t n) -> p t n", t=NT)
        places["eq4"] = taken[0]
        eq4 = part(NT * TOPK * E).rearrange("p (t k e) -> p t k e", t=NT, k=TOPK)
        eq4w = part(NT * TOPK * E).rearrange("p (t k e) -> p t k e", t=NT, k=TOPK)
        logit = part(NT * E).rearrange("p (t e) -> p t e", t=NT)
        chosen = part(NT * E).rearrange("p (t e) -> p t e", t=NT)
        combf = part(NT * E).rearrange("p (t e) -> p t e", t=NT)
        ranks = part(NT * E).rearrange("p (t e) -> p t e", t=NT)
        junk2 = (actT.rearrange("p c h s -> p (c h s)"),
                 arena[:, places["eq4"]:places["eq4"] + HALF])
        logitT = g1[:, 0:S]
        assert taken[0] <= first_end, (taken[0], first_end)
        top = sb("top", [P, NT, 8])
        topi = sb("topi", [P, NT, 8], U32)
        topf = sb("topf", [P, NT, 8])
        topw = sb("topw", [P, NT, TOPK])
        junk_o = sb("junk_o", [P, VD])
        scrap = sb("scrap", [P, 2])
        mask_q = sb("mask_q", [1, P], BF16)
        mask_k = sb("mask_k", [1, CHUNK], BF16)
        zrow = sb("zrow", [1, HALF], BF16)
        rounds_i = sb("rounds_i", [1, 1], I32)

        ss = small[:, 0:2]
        rstd = small[:, 2:4]
        qss = small[:, 8:40].rearrange("p (i g) -> p i g", i=4)
        qrs = small[:, 40:72].rearrange("p (i g) -> p i g", i=4)
        lam2 = small[:, 136:138]
        neglam = small[:, 138:139]
        mx = small[:, 140:144].rearrange("p (b m) -> p b m", b=2)
        den = small[:, 144:148].rearrange("p (b m) -> p b m", b=2)
        oss = small[:, 152:160]
        ors = small[:, 160:168]
        ngate = small[:, 168:184]
        bgate = cols[:, R_BGATE:R_BGATE + 2 * NC]
        subln8 = small[:, 184:185]
        psum4 = small[:, 188:190]
        ss2 = small[:, 196:200].rearrange("p (t h) -> p t h", t=NT)
        cnt = small[0:1, 192:193]
        cnt2 = small[0:1, 194:196]
        ropeb = sb("ropeb", [P, 8, 16])

        params = ([(gq, A["q_norm_g"][0:1, :].broadcast_to([P, HD])), (gk, A["k_norm_g"][0:1, :].broadcast_to([P, HD]))]
                  + [(lamv[:, i, :], A[n][0:1, :].broadcast_to([P, HD]))
                     for i, n in enumerate(("lambda_q1", "lambda_q2", "lambda_k1", "lambda_k2"))]
                  + [(poolw, A["pool_w"][0].rearrange("g c d -> c g d")),
                     (rw, A["router_w"][0].rearrange("(c p) e -> p c e", p=P)),
                     (rb, A["router_b"][0:1, :].broadcast_to([P, E]))])
        rows = [(R_MIXG, A["mix_norm_g"].rearrange("l (c p) -> (l c) p", p=P)),
                (R_BGATE, A["b_branch_gate"].rearrange("l (c p) -> (l c) p", p=P)),
                (R_PSCALE, A["pool_scale"].rearrange("l (c p) -> (l c) p", p=P)),
                (R_SUBLN, A["subln_g"]),
                (R_FFNG, A["ffn_norm_g"].rearrange("l (c p) -> (l c) p", p=P))]
        PARAMS = len(params)

        slot_in = [sem(f"slot_in{i}") for i in range(SLOTS)]
        piece_done = sem("piece_done")
        zero_col = sem("zero_col")
        x_in = [sem(f"x_in{t}") for t in range(NT)]
        x_again = sem("x_again")
        con_in = sem("con_in")
        rows_in = sem("rows_in")
        par_in = sem("par_in")
        out_done = sem("out_done")
        dve_step = sem("dve_step")
        pool_step = sem("pool_step")
        cols_T = sem("cols_T")
        cols_ready = sem("cols_ready")
        x_sq = sem("x_sq")
        x_var = sem("x_var")
        x_std = sem("x_std")
        h_ready = sem("h_ready")
        h_T = sem("h_T")
        hT_ready = sem("hT_ready")
        h_hi = sem("h_hi")
        h_lo = sem("h_lo")
        w_hi = sem("w_hi")
        w_lo = sem("w_lo")
        w_lo_pool = sem("w_lo_pool")
        y_hi = sem("y_hi")
        strip_done = sem("strip_done")
        strip_free = [sem("strip_free0"), sem("strip_free1")]
        qk_var = sem("qk_var")
        qk_std = sem("qk_std")
        qk_ready = sem("qk_ready")
        qk_T = sem("qk_T")
        q_moved = sem("q_moved")
        k_moved = sem("k_moved")
        pooled = sem("pooled")
        scored = sem("scored")
        max_ready = sem("max_ready")
        exp_ready = sem("exp_ready")
        diff_ready = sem("diff_ready")
        diff_T = sem("diff_T")
        diffT_ready = sem("diffT_ready")
        o_done = sem("o_done")
        o_ready = sem("o_ready")
        o_var = sem("o_var")
        o_std = sem("o_std")
        o_normed = sem("o_normed")
        o_T = sem("o_T")
        o_hi = sem("o_hi")
        o_lo = sem("o_lo")
        merged = sem("merged")
        m_hi = sem("m_hi")
        m_lo = sem("m_lo")
        wo_done = sem("wo_done")
        x2_ready = sem("x2_ready")
        x2_sq = sem("x2_sq")
        x2_var = sem("x2_var")
        x2_std = sem("x2_std")
        h2_ready = sem("h2_ready")
        x2_T = sem("x2_T")
        logit_done = sem("logit_done")
        top_ready = sem("top_ready")
        top_exp = sem("top_exp")
        rw_ready = sem("rw_ready")
        x2T_even = sem("x2T_even")
        x2T_odd = sem("x2T_odd")
        logitT_ready = sem("logitT_ready")
        logit_T = sem("logit_T")
        zero_row = sem("zero_row")
        mask_ready = sem("mask_ready")
        chosen_ready = sem("chosen_ready")
        rank_done = sem("rank_done")
        lam_exp = sem("lam_exp")
        lam_sum = sem("lam_sum")
        rounds_ready = sem("rounds_ready")
        pick_ready = sem("pick_ready")
        first_pick = sem("first_pick")
        gathered = sem("gathered")
        h_in_ready = sem("h_in_ready")
        g_ready = sem("g_ready")
        sig_ready = sem("sig_ready")
        act_ready = sem("act_ready")
        pick_T = sem("pick_T")
        pickT_ready = sem("pickT_ready")
        expert_step = sem("expert_step")
        hg_ready = sem("hg_ready")
        h_turned = sem("h_turned")
        act_T = sem("act_T")
        actT_ready = sem("actT_ready")
        y_ready = sem("y_ready")
        rows_zero = sem("rows_zero")
        bias_in = sem("bias_in")
        scattered = sem("scattered")
        out_ready = sem("out_ready")

        block = ctx.enter_context(nc.Block())

        w_in = A["w_in"][0].rearrange("(c p) n -> p c n", p=P)
        w_out = A["w_out"][0].rearrange("(c p) n -> p c n", p=P)

        def whole(w):
            return w.rearrange("(c p) n -> p c n", p=P)

        def cut(w, half):
            return w[:, :, HALF * half:HALF * (half + 1)]

        front = ([w_in[:, :, 512 + 512 * i:1024 + 512 * i] for i in range(3)] + [w_in[:, :, 0:512]]
                 + [w_in[:, :, 2048 + 512 * i:2560 + 512 * i] for i in range(2)]
                 + [whole(A["pool_up"][0])]
                 + [w_in[:, :, 3072 + 512 * i:3584 + 512 * i] for i in range(2)]
                 + [whole(A["attn_up"][0])] + [cut(w_out, 0), cut(w_out, 1)])
        Q_P, K_P, V_P, U_P, GA_P, PUP_P, GB_P, AUP_P, WO_P = 0, 1, 2, 3, 4, 6, 7, 9, 10
        FRONT = len(front)
        LAND, HIS, H_SLOT = 4, 3, 7
        SPLIT = [K_P, V_P, U_P, GA_P, GA_P + 1, PUP_P, GB_P, GB_P + 1, AUP_P, WO_P, WO_P + 1]
        BY_GPSIMD = (GA_P, GA_P + 1, PUP_P, GB_P)

        def hi_slot(n):
            return LAND + SPLIT.index(n) % HIS

        GB1, WO1 = GB_P + 1, WO_P + 1
        ORDER = [GB1 % LAND, H_SLOT, AUP_P % LAND, hi_slot(AUP_P), WO_P % LAND, hi_slot(WO_P), WO1 % LAND, hi_slot(WO1)]
        LEFT_BY = [GB1, GB1, AUP_P, AUP_P, WO_P, WO_P, WO1, WO1]
        assert sorted(ORDER) == list(range(SLOTS))
        BEFORE = [len([n for n in range(FRONT) if n % LAND == k]) for k in ORDER]

        def as_chunks(ap, wide):
            return ap.rearrange("p (c n) -> p c n", c=4 if wide else NC)

        def front_slot(n, wide=False):
            return as_chunks(ring[:, n % LAND, :], wide)

        def split_piece(n):
            return ring_r[hi_slot(n)][:], ring_r[n % LAND][:]

        def split_slot(n, wide=False):
            return tuple(as_chunks(ap, wide) for ap in split_piece(n))

        def slot(n):
            return as_chunks(ring[:, ORDER[n % SLOTS], :], True)

        h_split = tuple(ring_r[H_SLOT][:, NC * S * i:NC * S * (i + 1)].rearrange("p (c s) -> p c s", c=NC)
                        for i in range(2))
        PARTS = 4

        def lo_count(n, q):
            if n in BY_GPSIMD:
                return w_lo_pool, PARTS * BY_GPSIMD.index(n) + q + 1
            return w_lo, PARTS * [k for k in SPLIT if k not in BY_GPSIMD].index(n) + q + 1

        def quarter(ap, q):
            return ap[:, PIECE // PARTS * q:PIECE // PARTS * (q + 1)]

        units = [(t, h) for t in range(NT) for h in range(HEADS)]
        STEPS_ATT = len(units) + 2
        LATE = 3
        strips = ([("qkv", i) for i in range(6)] + [("u", g) for g in range(NG)]
                  + [("gate", c) for c in range(NC - 1)] + [("group", i) for i in range(2)] + [("gate", NC - 1)]
                  + [("pup", c) for c in range(NC)] + [("gate", NC + c) for c in range(NC)]
                  + [("aup", c) for c in range(NC)])
        strip_no = {s: n for n, s in enumerate(strips)}

        def strip_bank(s):
            return ps[:, strip_no[s] % 2, :]

        def strip_wait(eng, s):
            eng.wait_ge(strip_done, strip_no[s] + 1)

        def strip_release(ins, s):
            ins.then_inc(strip_free[strip_no[s] % 2], 1)

        def strip_read(eng, s):
            eng.wait_ge(strip_free[strip_no[s] % 2], strip_no[s] // 2 + 1)

        def front_piece_free(eng, n):
            last = {Q_P: ("qkv", 1), K_P: ("qkv", 3), V_P: ("qkv", 5), U_P: ("u", 3), GA_P: ("gate", 3),
                    GA_P + 1: ("gate", 7), PUP_P: ("pup", NC - 1), GB_P: ("gate", 11), GB_P + 1: ("gate", 15),
                    AUP_P: ("aup", NC - 1)}
            if n in last:
                strip_wait(eng, last[n])
            else:
                eng.wait_ge(wo_done, 2 + n - WO_P + 1)

        @block.sync
        def _(sp):
            for t in range(NT):
                sp.dma_start(xt[:, t, :], A["x"][0, P * t:P * (t + 1), :]).then_inc(x_in[t], 16)
            for r0, src in rows:
                sp.dma_start(prow[r0:r0 + src.shape[0], :], src).then_inc(rows_in, 16)
            for n, src in enumerate(front):
                if n == 1:
                    for dst, par in params:
                        sp.dma_start(dst, par).then_inc(par_in, 16)
                if n >= LAND:
                    front_piece_free(sp, n - LAND)
                sp.dma_start(front_slot(n, wide=src.shape[1] == 4), src).then_inc(slot_in[n % LAND], 16)
                if n == GB_P + 1:
                    sp.wait_ge(qk_T, 4)
                    for t in range(NT):
                        sp.dma_start(xt[:, t, :], A["x"][0, P * t:P * (t + 1), :]).then_inc(x_again, 16)

            def expert_pieces(step, at, first=False):
                for j in range(UNROLL):
                    for m, name in enumerate(("exp_w_gate", "exp_w_up", "exp_w_down")):
                        w = A[name][0].rearrange("e (c p) n -> p e c n", p=P)
                        for half in range(2):
                            n = PIECES_PER_EXPERT * j + 2 * m + half
                            if first and n < SLOTS:
                                front_piece_free(sp, LEFT_BY[n])
                            else:
                                sp.wait_ge(piece_done, at * (UNROLL * PIECES_PER_EXPERT) + (n - SLOTS + 1))
                            src = w[:, bass.ds(step * UNROLL + j, 1), 4 * half:4 * half + 4, :]
                            src = src.rearrange("p e c n -> p (e c) n")
                            sp.dma_start(slot(n), src).then_inc(slot_in[ORDER[n % SLOTS]], 16)

            expert_pieces(0, 0, first=True)
            with sp.Fori(1, STEPS) as step:
                expert_pieces(step, step)
            sp.wait_ge(rounds_ready, 1)
            rounds = sp.value_load(rounds_i[0:1, 0:1], min_val=1, max_val=ROUNDS)
            with sp.If(rounds > 1):
                with sp.Fori(1, rounds) as r:
                    with sp.Fori(0, STEPS) as step:
                        expert_pieces(step, r * STEPS + step)
            for t in range(NT):
                for half in range(2):
                    part_cols = slice(HALF * half, HALF * (half + 1))
                    sp.wait_ge(out_ready, 2 * t + half + 1)
                    sp.dma_start(out[0, P * t:P * (t + 1), part_cols], xt[:, t, part_cols]).then_inc(out_done, 16)
            sp.wait_ge(out_done, 16 * 2 * NT)

        @block.tensor
        def _(pe):
            mm, tr = nc.tensor.matmul, nc.tensor.transpose
            ALL = slice(None)

            def piece_wait(n):
                pe.wait_ge(slot_in[n % LAND], 16 * (n // LAND + 1))

            def split_wait(n, q):
                pe.wait_ge(w_hi, PARTS * SPLIT.index(n) + q + 1)
                pe.wait_ge(*lo_count(n, q))

            def mm3(dst, a, b, start, stop):
                mm(dst, a[0], b[1], start=start, stop=False)
                mm(dst, a[1], b[0], start=False, stop=False)
                return mm(dst, a[0], b[0], start=False, stop=stop)

            def both(ops, *at):
                return tuple(ap[at] for ap in ops)

            def strip_start(s):
                n = strip_no[s]
                if n >= 2:
                    pe.wait_ge(strip_free[n % 2], n // 2)

            pe.wait_ge(con_in, 16)
            pe.wait_ge(rows_in, 16 * 5)
            tr(ps[:, 0, 0:R_ROWS], prow[0:R_ROWS, :], ident[0:R_ROWS, 0:R_ROWS]).then_inc(cols_T, 1)
            for t in range(NT):
                pe.wait_ge(h_ready, t + 1)
                for q in range(2):
                    for c in range(4):
                        last = tr(ps[:, 2 + 2 * t + q, P * c:P * (c + 1)],
                                  xt[:, t, P * (4 * q + c):P * (4 * q + c + 1)], ident)
                    last.then_inc(h_T, 1)

            pe.wait_ge(cols_ready, 1)
            for i, piece in enumerate((Q_P, K_P, V_P)):
                for t in range(NT):
                    s = ("qkv", 2 * i + t)
                    strip_start(s)
                    tokens = slice(P * t, P * (t + 1))
                    if piece == Q_P:
                        piece_wait(piece)
                        pe.wait_ge(hT_ready, 2 * t + 2)
                    elif piece == K_P and t == 0:
                        pe.wait_ge(h_hi, 4)
                        pe.wait_ge(h_lo, 4)
                    for c in range(NC):
                        if piece == Q_P:
                            last = mm(strip_bank(s), hT[:, c, tokens], front_slot(piece)[:, c, :],
                                      start=(c == 0), stop=(c == NC - 1))
                            continue
                        if t == 0 and c % 2 == 0:
                            split_wait(piece, c // 2)
                        last = mm3(strip_bank(s), both(h_split, ALL, c, tokens), both(split_slot(piece), ALL, c),
                                   start=(c == 0), stop=(c == NC - 1))
                    last.then_inc(strip_done, 1)

            for w in range(2):
                pe.wait_ge(qk_ready, NT * (w + 1))
                for t in range(NT):
                    for h in range(HEADS):
                        last = tr(ps[:, 4 + 2 * w + t, P * h:P * (h + 1)], qk_tok[:, w, t, P * h:P * (h + 1)], ident)
                    last.then_inc(qk_T, 1)

            def by_channel(s, piece, cc):
                strip_start(s)
                columns = slice(P * cc, P * (cc + 1))
                dst = strip_bank(s)[:, 0:S]
                for c in range(NC):
                    if cc == 0 and c % 2 == 0:
                        split_wait(piece, c // 2)
                    last = mm3(dst, both(split_slot(piece), ALL, c, columns), both(h_split, ALL, c),
                               start=(c == 0), stop=(c == NC - 1))
                last.then_inc(strip_done, 1)

            def u_strip(g):
                by_channel(("u", g), U_P, g)

            def gate_strip(c):
                by_channel(("gate", c), (GA_P if c < NC else GB_P) + (c % NC) // 4, c % 4)

            def group_maps():
                pe.wait_ge(par_in, 16 * PARAMS)
                pe.wait_ge(pooled, NG)
                for i in range(2):
                    s = ("group", i)
                    strip_start(s)
                    for g in range(2):
                        last = mm(strip_bank(s)[:, S * g:S * (g + 1)], poolw[:, 2 * i + g, :], pT[:, 2 * i + g, :],
                                  start=True, stop=True)
                    last.then_inc(strip_done, 1)

            u_strip(0)
            u_strip(1)
            fill = [lambda: u_strip(2), lambda: u_strip(3)] + [lambda c=c: gate_strip(c) for c in range(NC)]

            for step in range(STEPS_ATT):
                if step < len(units):
                    t, h = units[step]
                    keys = P * (t + 1)
                    if step == 0:
                        pe.wait_ge(q_moved, 2)
                        pe.wait_ge(k_moved, 2)
                        pe.wait_ge(mask_ready, 3)
                    if step >= 2:
                        pe.wait_ge(exp_ready, 2 * (step - 1))
                    for m in range(2):
                        b = 4 + 2 * (step % 2) + m
                        rows = slice(HD * m, HD * (m + 1))
                        mm(ps[:, b, 0:keys], qT[rows, h, P * t:P * (t + 1)], kT[rows, h, 0:keys],
                           start=True, stop=True)
                    for m in range(2):
                        b = 4 + 2 * (step % 2) + m
                        last = mm(ps[:, b, keys - CHUNK:keys], mask_q[:], mask_k[:],
                                  start=False, stop=True, skip_group_check=True)
                    last.then_inc(scored, 1)
                fill[step]()
                if step == STEPS_ATT - 2:
                    group_maps()
                if 1 <= step <= len(units):
                    t, h = units[step - 1]
                    pe.wait_ge(diff_ready, step)
                    if step >= 2:
                        pe.wait_ge(diffT_ready, step - 1)
                    for kc in range(t + 1):
                        last = tr(ps[:, 2, P * kc:P * (kc + 1)], diff[:, (step - 1) % 2, P * kc:P * (kc + 1)], ident)
                    last.then_inc(diff_T, 1)
                if step >= 2:
                    t, h = units[step - 2]
                    pe.wait_ge(diffT_ready, step - 1)
                    if step == 2:
                        strip_read(pe, ("qkv", 4))
                        strip_read(pe, ("qkv", 5))
                    if step >= 3:
                        pe.wait_ge(o_ready, step - 2)
                    for kc in range(t + 1):
                        last = mm(ps[:, 3, 0:VD], diffT[:, step % 2, P * kc:P * (kc + 1)],
                                  vtok[:, kc, VD * h:VD * (h + 1)], start=(kc == 0), stop=(kc == t))
                    last.then_inc(o_done, 1)

            def up(kind, piece, src):
                for m in range(NC):
                    strip_start((kind, m))
                    for k in range(4):
                        if m == 0:
                            split_wait(piece, k)
                        last = mm3(strip_bank((kind, m))[:, 0:S],
                                   both(split_slot(piece, wide=True), ALL, k, slice(P * m, P * (m + 1))),
                                   both(src, ALL, k), start=(k == 0), stop=(k == 3))
                    last.then_inc(strip_done, 1)

            pe.wait_ge(y_hi, 2)
            strip_read(pe, ("group", 0))
            strip_read(pe, ("group", 1))
            up("pup", PUP_P, y_split)
            for c in range(NC, NC + 4):
                gate_strip(c)

            for t in range(NT):
                pe.wait_ge(o_normed, t + 1)
                for h in range(HEADS):
                    last = tr(ps[:, 2 + t, P * h:P * (h + 1)], otok[:, t, VD * h:VD * (h + 1)], ident)
                last.then_inc(o_T, 1)
            for c in range(NC + 4, 2 * NC):
                gate_strip(c)
            pe.wait_ge(o_hi, NT)
            pe.wait_ge(o_lo, NT)
            up("aup", AUP_P, o_split)

            def project(t, half):
                for m in range(NC):
                    if t == 0 and half == 0:
                        pe.wait_ge(m_hi, m + 1)
                        pe.wait_ge(m_lo, m + 1)
                    if t == 0 and m % 2 == 0:
                        split_wait(WO_P + half, m // 2)
                    last = mm3(ps[:, 4 + 2 * t + half, :], both(m_split, ALL, m, slice(P * t, P * (t + 1))),
                               both(split_slot(WO_P + half), ALL, m), start=(m == 0), stop=(m == NC - 1))
                last.then_inc(wo_done, 1)

            def turn_stream(t):
                for q in range(2):
                    pe.wait_ge(x2_ready, 2 * t + q + 1)
                    for c in range(4):
                        last = tr(ps[:, 2 * t + q, P * c:P * (c + 1)],
                                  xt[:, t, P * (4 * q + c):P * (4 * q + c + 1)], ident)
                    last.then_inc(x2_T, 1)

            project(0, 0)
            project(0, 1)
            project(1, 0)
            turn_stream(0)
            project(1, 1)
            turn_stream(1)
            pe.wait_ge(rw_ready, 1)
            pe.wait_ge(x2T_even, NT)
            pe.wait_ge(x2T_odd, NT)
            for k in range(2):
                for c in range(4):
                    last = mm(ps[E * c:E * (c + 1), 4, 0:S], rw[:, 4 * k + c, :], x2T[:, 4 * k + c, :],
                              start=(k == 0), stop=(k == 1))
            last.then_inc(logit_done, 1)
            pe.wait_ge(logitT_ready, 1)
            for t in range(NT):
                last = tr(ps[:, 6 + t, 0:P], logitT[:, P * t:P * (t + 1)], ident)
            last.then_inc(logit_T, 1)
            pe.wait_ge(zero_row, 1)
            for b in range(4):
                mm(ps[:, b, :], zrow[:, 0:P], zrow[:], start=True, stop=True)
            pe.wait_ge(chosen_ready, 1)
            mm(ps[:, 5, 0:E], tri, chosen[:, 0, :], start=True, stop=True)
            mm(ps[:, 5, E:2 * E], ones, chosen[:, 0, :], start=True, stop=False)
            mm(ps[:, 5, E:2 * E], tri, chosen[:, 1, :], start=False, stop=True).then_inc(rank_done, 1)
            for t in range(NT):
                last = mm(ps[0:1, 7, 0:E], ones[:, 0:1], chosen[:, t, :], start=(t == 0), stop=(t == NT - 1))
            last.then_inc(rank_done, 1)

            def gather(buf):
                for t in range(NT):
                    for half in range(2):
                        last = mm(ps[BLOCK * half:BLOCK * (half + 1), 6, :], pick[:, buf, t, :],
                                  h2[:, t, HALF * half:HALF * (half + 1)], start=(t == 0), stop=(t == NT - 1))
                last.then_inc(gathered, 1)

            def turn(bank, src):
                for c in range(4):
                    last = tr(ps[:, bank, P * c:P * (c + 1)], src[:, P * c:P * (c + 1)], ident)
                return last

            def scatter(signal=None):
                for t in range(NT):
                    for half in range(2):
                        rows = slice(BLOCK * half, BLOCK * (half + 1))
                        last = mm(ps[:, 2 * t + half, :], pickT[rows, P * t:P * (t + 1)], y_e[rows, :],
                                  start=False, stop=True, skip_group_check=True)
                        if signal:
                            last.then_inc(signal, 1)

            pe.wait_ge(first_pick, 1)
            pe.wait_ge(h2_ready, 2 * NT)
            gather(0)
            pe.wait_ge(pick_ready, 1)
            pe.wait_ge(hg_ready, 1)
            turn(6, h_got).then_inc(h_turned, 1)
            pe.wait_ge(rows_zero, 1)
            pe.wait_ge(bias_in, 16 * 3)

            pe.wait_ge(rounds_ready, 1)
            rounds = pe.value_load(rounds_i[0:1, 0:1], min_val=1, max_val=ROUNDS)
            with pe.Fori(0, rounds) as r:
                with pe.Fori(0, STEPS) as step:
                    done = (r * STEPS + step) * UNROLL
                    landed = (r * STEPS + step) * (16 * UNROLL * PIECES_PER_EXPERT // SLOTS)
                    for j in range(UNROLL):
                        buf = j % 2

                        def product(k, bank, src):
                            n = PIECES_PER_EXPERT * j + k
                            pe.wait_ge(slot_in[ORDER[n % SLOTS]], landed + 16 * (BEFORE[n % SLOTS] + n // SLOTS + 1))
                            for c in range(4):
                                for half in range(2):
                                    last = mm(ps[BLOCK * half:BLOCK * (half + 1), bank, :], src[:, c, k % 2, :],
                                              slot(n)[:, c, HALF * half:HALF * (half + 1)],
                                              start=False, stop=(k % 2 == 1 and c == 3))
                            last.then_inc(piece_done, 1)

                        def biases(k, bank):
                            for half in range(2):
                                mm(ps[BLOCK * half:BLOCK * (half + 1), bank, :], this_e[:, buf, k, :],
                                   bias_rows[:, HALF * half:HALF * (half + 1)], start=True, stop=False)

                        biases(0, 4)
                        pe.wait_ge(h_in_ready, done + (j + 1))
                        product(0, 4, h_in[:, buf])
                        product(1, 4, h_in[:, buf])
                        pe.wait_ge(y_ready, done + (j + 1))
                        pe.wait_ge(pickT_ready, done + (j + 1))
                        scatter()
                        biases(1, 5)
                        product(2, 5, h_in[:, buf])
                        product(3, 5, h_in[:, buf])
                        pe.wait_ge(pick_ready, done + (j + 2))
                        gather(1 - buf)
                        pe.wait_ge(act_ready, done + (j + 1))
                        turn(7, act_out).then_inc(act_T, 1)
                        for t in range(NT):
                            last = tr(ps[:, 5, P * t:P * (t + 1)], pickw[:, buf, t].rearrange("p h s -> p (h s)"), ident)
                        last.then_inc(pick_T, 1)
                        pe.wait_ge(hg_ready, done + (j + 2))
                        turn(6, h_got).then_inc(h_turned, 1)
                        pe.wait_ge(actT_ready, done + (j + 1))
                        biases(2, 7)
                        product(4, 7, actT)
                        product(5, 7, actT)
            pe.wait_ge(pickT_ready, rounds * E + 1)
            pe.wait_ge(y_ready, rounds * E + 1)
            scatter(signal=scattered)

        @block.scalar
        def _(act):
            fn = nc.scalar.activation
            act.dma_start(con[:], consts).then_inc(con_in, 16)
            act.wait_ge(zero_col, 1)
            fn(scrap[:, 1:2], scrap[:, 0:1], ACT.Sqrt)

            for t in range(NT):
                act.wait_ge(x_in[t], 16)
                fn(junk[:, t, :], xt[:, t, :], ACT.Square, accum_out=ss[:, t:t + 1]).then_inc(x_sq, 1)
            for t in range(NT):
                act.wait_ge(x_var, t + 1)
                fn(rstd[:, t:t + 1], rstd[:, t:t + 1], ACT.Sqrt).then_inc(x_std, 1)

            def hi_part(n, q):
                k = SPLIT.index(n)
                if q == 0:
                    act.wait_ge(slot_in[n % LAND], 16 * (n // LAND + 1))
                    if k >= HIS:
                        front_piece_free(act, SPLIT[k - HIS])
                hi, _lo = split_piece(n)
                nc.scalar.copy(quarter(hi, q), quarter(ring[:, n % LAND, :], q)).then_inc(w_hi, 1)

            def hi_parts(n):
                for q in range(PARTS):
                    hi_part(n, q)

            for t in range(NT):
                for q in range(2):
                    act.wait_ge(hT_ready, 2 * t + q + 1)
                    place = (slice(None), slice(4 * q, 4 * q + 4), slice(P * t, P * (t + 1)))
                    nc.scalar.copy(h_split[0][place], hT[place]).then_inc(h_hi, 1)
            hi_parts(K_P)

            for i in range(4):
                w, t = divmod(i, NT)
                if i == 2:
                    hi_parts(V_P)
                s = ("qkv", i)
                strip_wait(act, s)
                if t == 0 and w == 0:
                    act.wait_ge(h_T, 4)
                nc.scalar.copy(qk_tok[:, w, t, :], strip_bank(s))
                if i >= 2:
                    act.wait_ge(qk_var, i - 1)
                strip_release(fn(squares[:, i % 2, :], strip_bank(s), ACT.Square), s)
                act.wait_ge(qk_var, i + 1)
                fn(qrs[:, i, :], qrs[:, i, :], ACT.Sqrt).then_inc(qk_std, 1)
            hi_parts(U_P)
            for t in range(NT):
                s = ("qkv", 4 + t)
                strip_wait(act, s)
                strip_release(nc.scalar.copy(vtok[:, t, :], strip_bank(s)), s)
                for q in range(2):
                    hi_part(GA_P, 2 * t + q)
            act.wait_ge(lam_sum, 1)
            fn(lam2, lam2, ACT.Exp).then_inc(lam_exp, 1)
            for t in range(NT):
                act.wait_ge(qk_T, t + 1)
                nc.scalar.copy(qT[:, :, P * t:P * (t + 1)],
                               ps[:, 4 + t, :].rearrange("p (h s) -> p h s", h=HEADS)).then_inc(q_moved, 1)

            def u_copy(g):
                s = ("u", g)
                strip_wait(act, s)
                strip_release(nc.scalar.copy(uT[:, g, PAD:], strip_bank(s)[:, 0:S]), s)

            def gate_e(c):
                s = ("gate", c)
                strip_wait(act, s)
                strip_release(fn(gate[:, c, :], strip_bank(s)[:, 0:S], ACT.Exp, bias=ngate[:, c:c + 1], scale=-1.0), s)

            def gate_sigmoid(c):
                s = ("gate", c)
                strip_wait(act, s)
                strip_release(fn(gate[:, c, :], strip_bank(s)[:, 0:S], ACT.Sigmoid, bias=bgate[:, c:c + 1]), s)

            def group_hi():
                for i in range(2):
                    s = ("group", i)
                    strip_wait(act, s)
                    if i == 0:
                        act.wait_ge(pooled, NG)
                    for g in range(2):
                        last = fn(y_split[0][:, 2 * i + g, :], strip_bank(s)[:, S * g:S * (g + 1)], ACT.Copy,
                                  scale=cols[:, R_PSCALE + 2 * i + g:R_PSCALE + 2 * i + g + 1])
                    last.then_inc(y_hi, 1)

            u_copy(0)
            u_copy(1)
            ahead = [[(GA_P + 1, 2 * q), (GA_P + 1, 2 * q + 1)] for q in range(PARTS // 2)]
            ahead += [[(PUP_P, q)] for q in range(PARTS)] + [[(GB_P, 0)], [], [(GB_P, 1)], [(GB_P, 2), (GB_P, 3)]]
            fill = ([lambda: u_copy(2), lambda: u_copy(3)] + [lambda c=c: gate_e(c) for c in range(NC - LATE)]
                    + [lambda c=c: gate_sigmoid(c) for c in range(NC - LATE, NC)])
            for step in range(STEPS_ATT):
                b = step % 2
                if step < len(units):
                    t, h = units[step]
                    keys = P * (t + 1)
                    act.wait_ge(max_ready, step + 1)
                    for m in range(2):
                        fn(prob[:, b, m, 0:keys], ps[:, 4 + 2 * b + m, 0:keys], ACT.Exp, bias=mx[:, b, m:m + 1],
                           scale=HD ** -0.5, accum_out=den[:, b, m:m + 1]).then_inc(exp_ready, 1)
                fill[step]()
                if step == STEPS_ATT - 2:
                    group_hi()
                if 1 <= step <= len(units):
                    t, h = units[step - 1]
                    act.wait_ge(diff_T, step)
                    nc.scalar.copy(diffT[:, (step - 1) % 2, 0:P * (t + 1)], ps[:, 2, 0:P * (t + 1)]).then_inc(diffT_ready, 1)
                if step >= 2:
                    t, h = units[step - 2]
                    act.wait_ge(o_done, step - 1)
                    nc.scalar.copy(otok[:, t, VD * h:VD * (h + 1)], ps[:, 3, 0:VD])
                    fn(junk_o[:], ps[:, 3, 0:VD], ACT.Square, accum_out=oss[:, step - 2:step - 1]).then_inc(o_ready, 1)
                for n, q in ahead[step]:
                    hi_part(n, q)
            act.wait_ge(o_var, 1)
            fn(ors, ors, ACT.Sqrt).then_inc(o_std, 1)
            hi_parts(GB_P + 1)
            hi_parts(AUP_P)
            for c in range(NC, NC + 4):
                gate_sigmoid(c)
            for t in range(NT):
                act.wait_ge(o_T, t + 1)
                fn(o_split[0][:, :, P * t:P * (t + 1)], ps[:, 2 + t, :].rearrange("p (h s) -> p h s", h=HEADS), ACT.Copy,
                   scale=subln8).then_inc(o_hi, 1)
            hi_parts(WO_P)
            for c in range(NC + 4, 2 * NC):
                gate_sigmoid(c)
            hi_parts(WO_P + 1)
            for m in range(NC):
                act.wait_ge(merged, m + 1)
                nc.scalar.copy(m_split[0][:, m, :], gate[:, NC + m, :]).then_inc(m_hi, 1)

            def squares2(t, half):
                act.wait_ge(x2_ready, 2 * t + half + 1)
                fn(junk2[half], xt[:, t, HALF * half:HALF * (half + 1)], ACT.Square,
                   accum_out=ss2[:, t, half:half + 1]).then_inc(x2_sq, 1)

            def root2(t):
                act.wait_ge(x2_var, t + 1)
                fn(rstd[:, t:t + 1], rstd[:, t:t + 1], ACT.Sqrt).then_inc(x2_std, 1)

            def turned(t):
                act.wait_ge(x2_T, 2 * t + 2)
                nc.scalar.copy(x2T[:, 4:8, P * t:P * (t + 1)],
                               ps[:, 2 * t + 1, :].rearrange("p (c s) -> p c s", c=4)).then_inc(x2T_odd, 1)

            squares2(0, 0)
            for k, name in enumerate(("exp_b_gate", "exp_b_up", "exp_b_down")):
                act.dma_start(bias_rows[E * k:E * (k + 1), :], A[name][0]).then_inc(bias_in, 16)
            squares2(0, 1)
            root2(0)
            squares2(1, 0)
            turned(0)
            turned(1)
            squares2(1, 1)
            root2(1)
            act.wait_ge(logit_done, 1)
            nc.scalar.copy(logitT, ps[:, 4, 0:S]).then_inc(logitT_ready, 1)
            act.wait_ge(top_ready, 1)
            fn(topw[:], topw[:], ACT.Exp).then_inc(top_exp, 1)
            act.wait_ge(gathered, 1)
            nc.scalar.copy(h_got, ps[:, 6, :]).then_inc(hg_ready, 1)
            act.wait_ge(rounds_ready, 1)
            rounds = act.value_load(rounds_i[0:1, 0:1], min_val=1, max_val=ROUNDS)
            with act.Fori(0, rounds) as r:
                with act.Fori(0, STEPS) as step:
                    done = (r * STEPS + step) * UNROLL
                    for j in range(UNROLL):
                        act.wait_ge(g_ready, done + (j + 1))
                        fn(sig, g1, ACT.Sigmoid, scale=ALPHA).then_inc(sig_ready, 1)
                        act.wait_ge(gathered, done + (j + 2))
                        nc.scalar.copy(h_got, ps[:, 6, :]).then_inc(hg_ready, 1)
                        act.wait_ge(act_T, done + (j + 1))
                        nc.scalar.copy(actT.rearrange("p c h s -> p (c h s)"), ps[:, 7, :]).then_inc(actT_ready, 1)
                        act.wait_ge(pick_T, done + (j + 1))
                        nc.scalar.copy(pickT, ps[:, 5, 0:S]).then_inc(pickT_ready, 1)
                        act.wait_ge(piece_done, done * PIECES_PER_EXPERT + (PIECES_PER_EXPERT * j + 6))
                        nc.scalar.copy(y_e, ps[:, 7, :]).then_inc(y_ready, 1)

        @block.gpsimd
        def _(pool):
            steps = [0]

            def own(ins):
                steps[0] += 1
                ins.then_inc(pool_step, 1)
                pool.wait_ge(pool_step, steps[0])

            gp = nc.gpsimd
            own(gp.memset(uT[:, :, 0:PAD], 0.0))
            gp.memset(mask_q[:, 0:CHUNK], 1.0).then_inc(mask_ready, 1)
            gp.memset(mask_q[:, CHUNK:], 0.0).then_inc(mask_ready, 1)
            gp.memset(mask_k[:], MASKED).then_inc(mask_ready, 1)
            pool.wait_ge(mask_ready, 3)
            gp.memset(zrow[:], 0.0).then_inc(zero_row, 1)
            pool.wait_ge(zero_row, 1)
            pool.wait_ge(con_in, 16)

            def lo_parts(n):
                hi, lo = split_piece(n)
                for q in range(PARTS):
                    pool.wait_ge(w_hi, PARTS * SPLIT.index(n) + q + 1)
                    gp.tensor_tensor(quarter(lo, q), quarter(ring[:, n % LAND, :], q), quarter(hi, q).bitcast(F32),
                                     ALU.subtract).then_inc(w_lo_pool, 1)

            lo_parts(BY_GPSIMD[0])
            for g in range(NG):
                if g == NG // 2:
                    lo_parts(BY_GPSIMD[1])
                strip_read(pool, ("u", g))
                cur = uT[:, g, :]
                for k in range(g + 1):
                    lo, shift = (2 << k) - 1, 1 << k
                    nxt = sums[:, k % 2, :]
                    own(gp.tensor_tensor(nxt[:, lo:], cur[:, lo:], cur[:, lo - shift:S + PAD - shift], ALU.add))
                    cur = nxt
                gp.tensor_scalar(pT[:, g, 16:], cur[:, PAD + 16:], 1.0 / (2 << g), None, ALU.mult)
                own(gp.tensor_tensor(pT[:, g, 0:16], cur[:, PAD:PAD + 16], con[:, C_INV + 16 * g:C_INV + 16 * g + 16],
                                     ALU.mult))
                gp.tensor_tensor(pT[:, g, :], pT[:, g, :], uT[:, g, PAD:], ALU.subtract).then_inc(pooled, 1)
            for n in BY_GPSIMD[2:]:
                lo_parts(n)
            for m in range(NC):
                pool.wait_ge(m_hi, m + 1)
                gp.tensor_tensor(m_split[1][:, m, :], gate[:, NC + m, :], m_split[0][:, m, :].bitcast(F32),
                                 ALU.subtract).then_inc(m_lo, 1)
            pool.wait_ge(wo_done, 1)
            gp.memset(y_e, 0.0).then_inc(y_ready, 1)
            pool.wait_ge(y_ready, 1)
            gp.memset(pickT, 0.0).then_inc(pickT_ready, 1)
            pool.wait_ge(pickT_ready, 1)
            gp.memset(bias_rows[3 * E:, :], 0.0).then_inc(rows_zero, 1)

        @block.vector
        def _(dve):
            v = nc.vector
            steps = [0]

            def own(ins):
                steps[0] += 1
                ins.then_inc(dve_step, 1)
                dve.wait_ge(dve_step, steps[0])

            def wide(col, shape, axis):
                return col.unsqueeze(axis).broadcast_to(shape)

            v.memset(scrap[:, 0:1], 1.0).then_inc(zero_col, 1)
            for t in range(NT):
                dve.wait_ge(x_sq, t + 1)
                v.tensor_scalar(rstd[:, t:t + 1], ss[:, t:t + 1], 1.0 / D, EPS, ALU.mult, ALU.add).then_inc(x_var, 1)
            for t in range(NT):
                dve.wait_ge(x_std, t + 1)
                own(v.reciprocal(rstd[:, t:t + 1], rstd[:, t:t + 1]))
                v.tensor_scalar(xt[:, t, :], xt[:, t, :], rstd[:, t:t + 1], None, ALU.mult).then_inc(h_ready, 1)
            dve.wait_ge(cols_T, 1)
            v.tensor_copy(cols[:], ps[:, 0, 0:R_ROWS]).then_inc(cols_ready, 1)
            dve.wait_ge(cols_ready, 1)
            v.tensor_scalar(ngate, cols[:, R_BGATE:R_BGATE + 2 * NC], -1.0, None, ALU.mult)
            own(v.tensor_scalar(subln8, cols[:, R_SUBLN:R_SUBLN + 1], 1.0 - LAM_INIT, None, ALU.mult))
            for t in range(NT):
                for q in range(2):
                    dve.wait_ge(h_T, 2 * t + q + 1)
                    v.tensor_tensor(hT[:, 4 * q:4 * q + 4, P * t:P * (t + 1)],
                                    ps[:, 2 + 2 * t + q, :].rearrange("p (c s) -> p c s", c=4),
                                    wide(cols[:, R_MIXG + 4 * q:R_MIXG + 4 * q + 4], [P, 4, P], 2),
                                    ALU.mult).then_inc(hT_ready, 1)

            def minus(dst, whole_ap, hi):
                return v.tensor_tensor(dst, whole_ap, hi.bitcast(F32), ALU.subtract)

            def lo_part(n, q):
                dve.wait_ge(w_hi, PARTS * SPLIT.index(n) + q + 1)
                hi, lo = split_piece(n)
                minus(quarter(lo, q), quarter(ring[:, n % LAND, :], q), quarter(hi, q)).then_inc(w_lo, 1)

            def lo_parts(n):
                for q in range(PARTS):
                    lo_part(n, q)

            for t in range(NT):
                for q in range(2):
                    dve.wait_ge(h_hi, 2 * t + q + 1)
                    place = (slice(None), slice(4 * q, 4 * q + 4), slice(P * t, P * (t + 1)))
                    minus(h_split[1][place], hT[place], h_split[0][place]).then_inc(h_lo, 1)
            lo_parts(K_P)
            dve.wait_ge(par_in, 16 * PARAMS)
            own(v.tensor_tensor(lamv[:, 0:2, :], lamv[:, 0:2, :], lamv[:, 2:4, :], ALU.mult))
            v.tensor_reduce(lam2, lamv[:, 0:2, :], AX.X, ALU.add).then_inc(lam_sum, 1)

            for i in range(4):
                w, t = divmod(i, NT)
                if i == 2:
                    lo_parts(V_P)
                strip_read(dve, ("qkv", i))
                own(v.tensor_reduce(qss[:, i, :], squares[:, i % 2, :].rearrange("p (g d) -> p g d", d=HD), AX.X, ALU.add))
                v.tensor_scalar(qrs[:, i, :], qss[:, i, :], 1.0 / HD, EPS, ALU.mult, ALU.add).then_inc(qk_var, 1)
                dve.wait_ge(qk_std, i + 1)
                own(v.reciprocal(qrs[:, i, :], qrs[:, i, :]))
                z = qk_tok[:, w, t, :].rearrange("p (g d) -> p g d", d=HD)
                own(v.tensor_tensor(z, z, wide(qrs[:, i, :], [P, 8, HD], 2), ALU.mult))
                own(v.tensor_tensor(z, z, wide((gq, gk)[w], [P, 8, HD], 1), ALU.mult))
                cosb = wide(con[:, C_COS + 8 * t:C_COS + 8 * t + 8], [P, 8, 8], 1)
                sinb = wide(con[:, C_SIN + 8 * t:C_SIN + 8 * t + 8], [P, 8, 8], 1)
                v.tensor_tensor(ropeb[:, :, 0:8], z[:, :, 8:16], sinb, ALU.mult)
                own(v.tensor_tensor(ropeb[:, :, 8:16], z[:, :, 0:8], sinb, ALU.mult))
                v.tensor_tensor(z[:, :, 0:8], z[:, :, 0:8], cosb, ALU.mult)
                own(v.tensor_tensor(z[:, :, 8:16], z[:, :, 8:16], cosb, ALU.mult))
                own(v.tensor_tensor(z[:, :, 0:8], z[:, :, 0:8], ropeb[:, :, 0:8], ALU.subtract))
                v.tensor_tensor(z[:, :, 8:16], z[:, :, 8:16], ropeb[:, :, 8:16], ALU.add).then_inc(qk_ready, 1)
            lo_parts(U_P)
            for t in range(NT):
                dve.wait_ge(qk_T, NT + t + 1)
                v.tensor_copy(kT[:, :, P * t:P * (t + 1)],
                              ps[:, 6 + t, :].rearrange("p (h s) -> p h s", h=HEADS)).then_inc(k_moved, 1)
            dve.wait_ge(lam_exp, 1)
            own(v.tensor_tensor(neglam, lam2[:, 1:2], lam2[:, 0:1], ALU.subtract))
            own(v.tensor_scalar(neglam, neglam, -LAM_INIT, None, ALU.add))

            def sigmoid_rest(c):
                strip_read(dve, ("gate", c))
                own(v.tensor_scalar(gate[:, c, :], gate[:, c, :], 1.0, None, ALU.add))
                return v.reciprocal(gate[:, c, :], gate[:, c, :])

            for step in range(len(units)):
                t, h = units[step]
                b, keys = step % 2, P * (t + 1)
                dve.wait_ge(scored, step + 1)
                own(v.tensor_reduce(mx[:, b, :], ps[:, 4 + 2 * b:6 + 2 * b, 0:keys], AX.X, ALU.max))
                v.tensor_scalar(mx[:, b, :], mx[:, b, :], -HD ** -0.5, None, ALU.mult).then_inc(max_ready, 1)
                if step >= LATE:
                    own(sigmoid_rest(step - LATE))
                dve.wait_ge(exp_ready, 2 * step + 2)
                own(v.reciprocal(den[:, b, :], den[:, b, :]))
                own(v.tensor_tensor(den[:, b, 1:2], den[:, b, 1:2], neglam, ALU.mult))
                own(v.tensor_scalar(prob[:, b, 1, 0:keys], prob[:, b, 1, 0:keys], den[:, b, 1:2], None, ALU.mult))
                v.scalar_tensor_tensor(out=diff[:, b, 0:keys], in0=prob[:, b, 0, 0:keys], scalar=den[:, b, 0:1],
                                       in1=prob[:, b, 1, 0:keys], op0=ALU.mult, op1=ALU.add).then_inc(diff_ready, 1)
            for i in range(2):
                s = ("group", i)
                dve.wait_ge(y_hi, i + 1)
                for g in range(2):
                    k = 2 * i + g
                    last = v.scalar_tensor_tensor(out=y_split[1][:, k, :], in0=strip_bank(s)[:, S * g:S * (g + 1)],
                                                  scalar=cols[:, R_PSCALE + k:R_PSCALE + k + 1],
                                                  in1=y_split[0][:, k, :].bitcast(F32), op0=ALU.mult, op1=ALU.subtract)
                strip_release(last, s)
            dve.wait_ge(o_ready, len(units))
            v.tensor_scalar(ors, oss, 1.0 / VD, EPS, ALU.mult, ALU.add).then_inc(o_var, 1)

            def head_norms():
                dve.wait_ge(o_std, 1)
                own(v.reciprocal(ors, ors))
                for t in range(NT):
                    z = otok[:, t, :].rearrange("p (h d) -> p h d", h=HEADS)
                    v.tensor_tensor(z, z, wide(ors[:, HEADS * t:HEADS * (t + 1)], [P, HEADS, VD], 2),
                                    ALU.mult).then_inc(o_normed, 1)

            for m in range(NC):
                s = ("pup", m)
                strip_wait(dve, s)
                if m >= NC - LATE:
                    strip_read(dve, ("gate", m))
                strip_release(v.tensor_tensor(gate[:, m, :], strip_bank(s)[:, 0:S], gate[:, m, :], ALU.mult), s)
                if m == 1:
                    head_norms()
            lo_parts(GB_P + 1)
            lo_parts(AUP_P)
            for t in range(NT):
                dve.wait_ge(o_hi, t + 1)
                part_t = (slice(None), slice(None), slice(P * t, P * (t + 1)))
                v.scalar_tensor_tensor(out=o_split[1][part_t], in0=ps[:, 2 + t, :].rearrange("p (h s) -> p h s", h=HEADS),
                                       scalar=subln8, in1=o_split[0][part_t].bitcast(F32), op0=ALU.mult,
                                       op1=ALU.subtract).then_inc(o_lo, 1)
            lo_parts(WO_P)

            for m in range(NC):
                s = ("aup", m)
                strip_wait(dve, s)
                strip_read(dve, ("gate", NC + m))
                strip_release(v.tensor_tensor(gate[:, NC + m, :], strip_bank(s)[:, 0:S], gate[:, NC + m, :], ALU.mult), s)
                strip_read(dve, s)
                v.tensor_tensor(gate[:, NC + m, :], gate[:, m, :], gate[:, NC + m, :], ALU.add).then_inc(merged, 1)
            lo_parts(WO_P + 1)

            dve.wait_ge(x_again, 16 * NT)

            def residual(t, half):
                dve.wait_ge(wo_done, 2 * t + half + 1)
                z = xt[:, t, HALF * half:HALF * (half + 1)]
                v.tensor_tensor(z, z, ps[:, 4 + 2 * t + half, :], ALU.add).then_inc(x2_ready, 1)

            def normed(t):
                dve.wait_ge(x2_sq, 2 * t + 2)
                own(v.tensor_tensor(ss[:, t:t + 1], ss2[:, t, 0:1], ss2[:, t, 1:2], ALU.add))
                v.tensor_scalar(rstd[:, t:t + 1], ss[:, t:t + 1], 1.0 / D, EPS, ALU.mult, ALU.add).then_inc(x2_var, 1)
                dve.wait_ge(x2_std, t + 1)
                own(v.reciprocal(rstd[:, t:t + 1], rstd[:, t:t + 1]))
                for half in range(2):
                    part_cols = slice(HALF * half, HALF * (half + 1))
                    v.tensor_scalar(h2[:, t, part_cols], xt[:, t, part_cols], rstd[:, t:t + 1], None,
                                    ALU.mult).then_inc(h2_ready, 1)

            def turned(t):
                dve.wait_ge(x2_T, 2 * t + 1)
                v.tensor_copy(x2T[:, 0:4, P * t:P * (t + 1)],
                              ps[:, 2 * t, :].rearrange("p (c s) -> p c s", c=4)).then_inc(x2T_even, 1)

            residual(0, 0)
            residual(0, 1)
            normed(0)
            v.tensor_tensor(rw, rw, wide(cols[:, R_FFNG:R_FFNG + NC], [P, NC, E], 2), ALU.mult).then_inc(rw_ready, 1)
            residual(1, 0)
            turned(0)
            residual(1, 1)
            turned(1)
            normed(1)

            dve.wait_ge(logit_T, 1)
            own(v.tensor_reduce(logit, ps[:, 6:8, 0:P].rearrange("p t (g e) -> p t e g", g=4), AX.X, ALU.add))
            for t in range(NT):
                last = v.scalar_tensor_tensor(out=logit[:, t, :], in0=logit[:, t, :], scalar=rstd[:, t:t + 1], in1=rb,
                                              op0=ALU.mult, op1=ALU.add)
            own(last)
            for t in range(NT):
                last = v.max(top[:, t, :], logit[:, t, :])
            own(last)
            v.tensor_tensor(topw[:], top[:, :, 0:TOPK], top[:, :, 0:1].broadcast_to([P, NT, TOPK]),
                            ALU.subtract).then_inc(top_ready, 1)
            for t in range(NT):
                last = v.max_index(topi[:, t, :], top[:, t, :], logit[:, t, :])
            own(last)
            own(v.tensor_copy(topf[:], topi[:]))
            for t in range(NT):
                last = v.tensor_tensor(eq4[:, t], wide(iota[:, 0:E], [P, TOPK, E], 1),
                                       wide(topf[:, t, 0:TOPK], [P, TOPK, E], 2), ALU.is_equal)
            own(last)
            v.tensor_reduce(chosen, eq4.rearrange("p t k e -> p t e k"), AX.X, ALU.add).then_inc(chosen_ready, 1)
            dve.wait_ge(top_exp, 1)
            own(v.tensor_reduce(psum4, topw[:], AX.X, ALU.add))
            own(v.reciprocal(psum4, psum4))
            own(v.tensor_tensor(topw[:], topw[:], wide(psum4, [P, NT, TOPK], 2), ALU.mult))
            dve.wait_ge(rank_done, 1)
            own(v.tensor_tensor(ranks, ps[:, 5, 0:2 * E].rearrange("p (t e) -> p t e", t=NT), chosen, ALU.mult))

            def rank_block(r):
                return v.tensor_scalar(rank_tab[:, :, E * r:E * (r + 1)], ranks, -1.0 - BLOCK * r, None, ALU.add)

            own(rank_block(0))

            def select(n, buf):
                for t in range(NT):
                    last = v.tensor_scalar(pick[:, buf, t, :], iota, rank_tab[:, t, bass.ds(n, 1)], None, ALU.is_equal)
                return last

            def weigh(n, buf):
                for t in range(NT):
                    v.tensor_scalar(pickw[:, buf, t], wide(iota, [P, 2, BLOCK], 1), rank_tab[:, t, bass.ds(n, 1)],
                                    comb_tab[:, t, bass.ds(n, 1)], ALU.is_equal, ALU.mult)

            def name_expert(e, buf):
                for k in range(3):
                    last = v.tensor_copy(this_e[:, buf, k, :],
                                         con[:, bass.ds(e + (C_IDENT + E * k), 1)].broadcast_to([P, BLOCK]))
                last.then_inc(pick_ready, 1)

            select(0, 0).then_inc(first_pick, 1)
            name_expert(0, 0)
            for r in range(1, ROUNDS + 1):
                last = rank_block(r)
            own(last)
            dve.wait_ge(rank_done, 2)
            own(v.tensor_reduce(cnt, ps[0:1, 7, 0:E], AX.X, ALU.max))
            own(v.tensor_scalar(cnt2[:, 0:1], cnt, float(BLOCK), 1.0, ALU.is_gt, ALU.add))
            own(v.scalar_tensor_tensor(out=cnt2[:, 1:2], in0=cnt, scalar=2.0 * BLOCK, in1=cnt2[:, 0:1],
                                       op0=ALU.is_gt, op1=ALU.add))
            v.scalar_tensor_tensor(out=rounds_i[:], in0=cnt, scalar=3.0 * BLOCK, in1=cnt2[:, 1:2],
                                   op0=ALU.is_gt, op1=ALU.add).then_inc(rounds_ready, 1)

            for t in range(NT):
                last = v.tensor_tensor(eq4w[:, t], eq4[:, t], wide(topw[:, t, :], [P, TOPK, E], 2), ALU.mult)
            own(last)
            own(v.tensor_reduce(combf, eq4w.rearrange("p t k e -> p t e k"), AX.X, ALU.add))
            own(v.tensor_copy(comb_tab.rearrange("p t (r e) -> p t r e", e=E),
                          combf.unsqueeze(2).broadcast_to([P, NT, ROUNDS + 1, E])))
            weigh(0, 0)

            def gathered_in(buf):
                gain = cols[:, R_FFNG:R_FFNG + NC].rearrange("p (h c) -> p c h", h=2)
                v.tensor_tensor(h_in[:, buf], ps[:, 6, :].rearrange("p (c h s) -> p c h s", c=4, h=2),
                                wide(gain, [P, 4, 2, BLOCK], 3), ALU.mult).then_inc(h_in_ready, 1)

            dve.wait_ge(h_turned, 1)
            gathered_in(0)

            dve.wait_ge(rounds_ready, 1)
            rounds = dve.value_load(rounds_i[0:1, 0:1], min_val=1, max_val=ROUNDS)
            with dve.Fori(0, rounds) as r:
                with dve.Fori(0, STEPS) as step:
                    done = (r * STEPS + step) * UNROLL
                    after = ((step + 1) & (STEPS - 1)) * UNROLL
                    for j in range(UNROLL):
                        dve.wait_ge(piece_done, done * PIECES_PER_EXPERT + (PIECES_PER_EXPERT * j + 2))
                        v.tensor_scalar(g1, ps[:, 4, :], LIMIT, None, ALU.min).then_inc(g_ready, 1)
                        e = (step * UNROLL + (j + 1)) if j < UNROLL - 1 else after
                        select(done + (j + 1), 1 - j % 2)
                        weigh(done + (j + 1), 1 - j % 2)
                        name_expert(e, 1 - j % 2)
                        dve.wait_ge(sig_ready, done + (j + 1))
                        v.tensor_tensor(gs, g1, sig, ALU.mult).then_inc(expert_step, 1)
                        dve.wait_ge(piece_done, done * PIECES_PER_EXPERT + (PIECES_PER_EXPERT * j + 4))
                        v.tensor_scalar(u1, ps[:, 5, :], LIMIT, -LIMIT, ALU.min, ALU.max).then_inc(expert_step, 1)
                        dve.wait_ge(expert_step, done * 2 + (2 * j + 2))
                        v.scalar_tensor_tensor(out=act_out, in0=u1, scalar=1.0, in1=gs, op0=ALU.add,
                                               op1=ALU.mult).then_inc(act_ready, 1)
                        dve.wait_ge(h_turned, done + (j + 2))
                        gathered_in(1 - j % 2)
            for t in range(NT):
                for half in range(2):
                    dve.wait_ge(scattered, 2 * t + half + 1)
                    z = xt[:, t, HALF * half:HALF * (half + 1)]
                    v.tensor_tensor(z, z, ps[:, 2 * t + half, :], ALU.add).then_inc(out_ready, 1)


_INS = ["x", "mix_norm_g", "w_in", "b_branch_gate", "pool_w", "pool_scale", "pool_up", "q_norm_g", "k_norm_g",
        "lambda_q1", "lambda_k1", "lambda_q2", "lambda_k2", "subln_g", "attn_up", "w_out", "ffn_norm_g",
        "router_w", "router_b", "exp_w_gate", "exp_b_gate", "exp_w_up", "exp_b_up", "exp_w_down", "exp_b_down"]


def kernel(**inputs):
    import concourse.bacc as _bacc
    from concourse.bass_utils import run_bass_kernel_spmd as _run

    nc = _bacc.Bacc("TRN2", target_bir_lowering=False, num_devices=1)
    arrays, aps = {}, {}
    for name in _INS:
        a = np.ascontiguousarray(inputs[name])
        arrays["in_" + name] = a
        aps[name] = nc.dram_tensor("in_" + name, a.shape, mybir.dt.from_np(a.dtype), kind="ExternalInput").ap()
    arrays["shape_constants"] = shape_constants()
    consts = nc.dram_tensor("shape_constants", (P, C_WIDTH), F32, kind="ExternalInput").ap()
    out = nc.dram_tensor("out", (1, S, D), F32, kind="ExternalOutput").ap()
    build(nc, aps, consts, out)
    r = _run(nc, [arrays], core_ids=[0])
    return r.results[0]["out"]
```
